# Optimizing a Trainium2 kernel written in Bass

```python
import math
import jax, jax.numpy as jnp
from jax import lax
import numpy as np

D_MODEL = 1024
BATCH = 1
SEQ = 512
DEPTH = 2

CHUNK = 64
N_META = 16
N_A = DEPTH // 2
N_B = DEPTH - N_A
D_FF = 2816
POOL_WINDOWS = (2, 4, 8, 16)
N_POOL_GROUPS = len(POOL_WINDOWS)
POOL_GROUP = D_MODEL // N_POOL_GROUPS
N_HEADS = 8
QK_NOPE = 64
QK_ROPE = 32
V_HEAD = 64
KV_RANK = 256
Q_RANK = 384
ROPE_THETA = 10000.0
Q_BLOCK = 128
EPS = 1e-6


def rmsnorm(x, g):
    xf = x.astype(jnp.float32)
    xf = xf * lax.rsqrt(jnp.mean(xf * xf, axis=-1, keepdims=True) + EPS)
    return xf.astype(x.dtype) * g

def swiglu(h, w_gate, w_up, w_down):
    return (jax.nn.silu(h @ w_gate) * (h @ w_up)) @ w_down

def chunk_ids(n):
    pos = jnp.arange(n)
    return jnp.where(pos < N_META, 0, (pos - N_META) // CHUNK + 1)

def rope_tables(n):
    inv = 1.0 / (ROPE_THETA ** (jnp.arange(0, QK_ROPE, 2, dtype=jnp.float32) / QK_ROPE))
    ang = jnp.arange(n, dtype=jnp.float32)[:, None] * inv[None, :]
    return jnp.cos(ang), jnp.sin(ang)

def apply_rope(x, cos, sin):
    xf = x.astype(jnp.float32)
    x1, x2 = xf[..., : QK_ROPE // 2], xf[..., QK_ROPE // 2:]
    out = jnp.concatenate([x1 * cos - x2 * sin, x2 * cos + x1 * sin], axis=-1)
    return out.astype(x.dtype)

def pool_mixer(h, w_group, scale):
    L = h.shape[1]
    hf = h.astype(jnp.float32)
    cs = jnp.concatenate([jnp.zeros_like(hf[:, :1]), jnp.cumsum(hf, axis=1)], axis=1)
    hi = jnp.arange(1, L + 1)
    outs = []
    for g, w in enumerate(POOL_WINDOWS):
        sl = slice(g * POOL_GROUP, (g + 1) * POOL_GROUP)
        lo = jnp.maximum(hi - w, 0)
        c = cs[..., sl]
        count = (hi - lo).astype(jnp.float32)[None, :, None]
        mean = (jnp.take(c, hi, axis=1) - jnp.take(c, lo, axis=1)) / count
        outs.append(mean - hf[..., sl])
    pooled = jnp.stack(outs, axis=2).astype(h.dtype)
    y = jnp.einsum('blgc,gcd->blgd', pooled, w_group)
    return y.reshape(h.shape) * scale

def mla_shared_kv(h, w_dkv, kv_latent_norm, w_uk, w_uv, cos, sin):
    B, L, _ = h.shape
    ckr = h @ w_dkv
    c_kv = rmsnorm(ckr[..., :KV_RANK], kv_latent_norm)
    k_rope = apply_rope(ckr[..., KV_RANK:], cos, sin)
    k_nope = (c_kv @ w_uk).reshape(B, L, N_HEADS, QK_NOPE)
    v = (c_kv @ w_uv).reshape(B, L, N_HEADS, V_HEAD)
    return k_nope, k_rope, v

def mla_attention(h, w_dq, q_latent_norm, w_uq, w_o, k_nope, k_rope, v, cos, sin):
    B, L, _ = h.shape
    cq = rmsnorm(h @ w_dq, q_latent_norm)
    q = (cq @ w_uq).reshape(B, L, N_HEADS, QK_NOPE + QK_ROPE)
    q_nope = q[..., :QK_NOPE]
    q_rope = apply_rope(q[..., QK_NOPE:], cos[:, None, :], sin[:, None, :])
    n_blk = -(-L // Q_BLOCK)
    Lp = n_blk * Q_BLOCK
    pad = ((0, 0), (0, Lp - L), (0, 0), (0, 0))
    qn_b = jnp.pad(q_nope, pad).reshape(B, n_blk, Q_BLOCK, N_HEADS, QK_NOPE).transpose(1, 0, 2, 3, 4)
    qr_b = jnp.pad(q_rope, pad).reshape(B, n_blk, Q_BLOCK, N_HEADS, QK_ROPE).transpose(1, 0, 2, 3, 4)
    qid_b = chunk_ids(Lp).reshape(n_blk, Q_BLOCK)
    kid = chunk_ids(L)
    sm_scale = 1.0 / math.sqrt(QK_NOPE + QK_ROPE)

    def block(args):
        qn, qr, qid = args
        s = (jnp.einsum('bqhd,bkhd->bhqk', qn, k_nope)
             + jnp.einsum('bqhr,bkr->bhqk', qr, k_rope)).astype(jnp.float32) * sm_scale
        mask = kid[None, :] <= qid[:, None]
        s = jnp.where(mask[None, None], s, jnp.finfo(jnp.float32).min)
        p = jax.nn.softmax(s, axis=-1).astype(v.dtype)
        return jnp.einsum('bhqk,bkhd->bqhd', p, v)

    o = lax.map(block, (qn_b, qr_b, qid_b))
    o = o.transpose(1, 0, 2, 3, 4).reshape(B, Lp, N_HEADS * V_HEAD)[:, :L]
    return o @ w_o

def first_inputs(seed: int = 0) -> dict:
    key = jax.random.key(seed)
    ks = iter(jax.random.split(key, 40))
    f32 = jnp.float32

    def nrm(shape, fan_in):
        return jax.random.normal(next(ks), shape, f32) * (fan_in ** -0.5)

    def gain(shape):
        return 1.0 + 0.1 * jax.random.normal(next(ks), shape, f32)

    return {
        "x": jax.random.normal(next(ks), (BATCH, SEQ, D_MODEL), f32),
        "meta_tokens": jax.random.normal(next(ks), (N_META, D_MODEL), f32),
        "ffn1_norm": gain((DEPTH, D_MODEL)),
        "ffn1_w_gate": nrm((DEPTH, D_MODEL, D_FF), D_MODEL),
        "ffn1_w_up": nrm((DEPTH, D_MODEL, D_FF), D_MODEL),
        "ffn1_w_down": nrm((DEPTH, D_FF, D_MODEL), D_FF),
        "mix_norm": gain((DEPTH, D_MODEL)),
        "ffn2_norm": gain((DEPTH, D_MODEL)),
        "ffn2_w_gate": nrm((DEPTH, D_MODEL, D_FF), D_MODEL),
        "ffn2_w_up": nrm((DEPTH, D_MODEL, D_FF), D_MODEL),
        "ffn2_w_down": nrm((DEPTH, D_FF, D_MODEL), D_FF),
        "pool_w": nrm((N_A, N_POOL_GROUPS, POOL_GROUP, POOL_GROUP), POOL_GROUP),
        "pool_scale": gain((N_A, D_MODEL)),
        "kv_in_norm": gain((D_MODEL,)),
        "w_dkv": nrm((D_MODEL, KV_RANK + QK_ROPE), D_MODEL),
        "kv_latent_norm": gain((KV_RANK,)),
        "w_uk": nrm((KV_RANK, N_HEADS * QK_NOPE), KV_RANK),
        "w_uv": nrm((KV_RANK, N_HEADS * V_HEAD), KV_RANK),
        "w_dq": nrm((N_B, D_MODEL, Q_RANK), D_MODEL),
        "q_latent_norm": gain((N_B, Q_RANK)),
        "w_uq": nrm((N_B, Q_RANK, N_HEADS * (QK_NOPE + QK_ROPE)), Q_RANK),
        "w_o": nrm((N_B, N_HEADS * V_HEAD, D_MODEL), N_HEADS * V_HEAD),
        "final_norm": gain((D_MODEL,)),
    }

def first_block(x, meta_tokens, ffn1_norm, ffn1_w_gate, ffn1_w_up, ffn1_w_down, mix_norm,
              ffn2_norm, ffn2_w_gate, ffn2_w_up, ffn2_w_down, pool_w, pool_scale,
              kv_in_norm, w_dkv, kv_latent_norm, w_uk, w_uv, w_dq, q_latent_norm, w_uq, w_o,
              final_norm):
    B = x.shape[0]
    meta = jnp.broadcast_to(meta_tokens[None].astype(x.dtype), (B, N_META, D_MODEL))
    h = jnp.concatenate([meta, x], axis=1)
    L = h.shape[1]
    cos, sin = rope_tables(L)
    shared = None
    for l in range(DEPTH):
        h = h + 0.5 * swiglu(rmsnorm(h, ffn1_norm[l]), ffn1_w_gate[l], ffn1_w_up[l], ffn1_w_down[l])
        u = rmsnorm(h, mix_norm[l])
        if l < N_A:
            h = h + pool_mixer(u, pool_w[l], pool_scale[l])
        else:
            j = l - N_A
            k_nope, k_rope, v = shared
            h = h + mla_attention(u, w_dq[j], q_latent_norm[j], w_uq[j], w_o[j],
                                  k_nope, k_rope, v, cos, sin)
        h = h + 0.5 * swiglu(rmsnorm(h, ffn2_norm[l]), ffn2_w_gate[l], ffn2_w_up[l], ffn2_w_down[l])
        if l == N_A - 1:
            shared = mla_shared_kv(rmsnorm(h, kv_in_norm), w_dkv, kv_latent_norm, w_uk, w_uv, cos, sin)
    out = rmsnorm(h, final_norm)
    return out[:, N_META:]


DEPTH_2 = 1

HEAD_DIM = 64
W_ATTN = N_HEADS * HEAD_DIM
C_CONF = D_MODEL // 2
CONF_WIDTH = 31
C_SC = D_MODEL // 2
SC_WIDTH = 3
N_BRANCH = 3
D_FF_2 = ((8 * D_MODEL + 2) // 3 + 255) // 256 * 256
BLOCK_Q = 128
SPLIT_SIZES = (W_ATTN, W_ATTN, W_ATTN, C_CONF, C_CONF, C_SC, C_SC, C_SC, N_BRANCH * D_MODEL)
SPLIT_IDX = tuple(int(i) for i in np.cumsum(SPLIT_SIZES)[:-1])
N_IN = int(sum(SPLIT_SIZES))


def rms_norm(x, g):
    xf = x.astype(jnp.float32)
    y = xf * lax.rsqrt(jnp.mean(xf * xf, axis=-1, keepdims=True) + EPS)
    return (y * g.astype(jnp.float32)).astype(x.dtype)

def layer_norm(x, g, b):
    xf = x.astype(jnp.float32)
    mu = jnp.mean(xf, axis=-1, keepdims=True)
    var = jnp.mean(jnp.square(xf - mu), axis=-1, keepdims=True)
    y = (xf - mu) * lax.rsqrt(var + EPS)
    return (y * g.astype(jnp.float32) + b.astype(jnp.float32)).astype(x.dtype)

def causal_depthwise_conv(x, w):
    width, ch = w.shape
    return lax.conv_general_dilated(
        x, w[:, None, :].astype(x.dtype), window_strides=(1,), padding=[(width - 1, 0)],
        dimension_numbers=("NWC", "WIO", "NWC"), feature_group_count=ch)

def stick_breaking_attention(q, k, v):
    b, h, s, dh = q.shape
    nb = s // BLOCK_Q
    scale = float(1.0 / np.sqrt(dh))
    qb = q.reshape(b, h, nb, BLOCK_Q, dh).transpose(2, 0, 1, 3, 4)
    kpos = jnp.arange(s)

    def one_block(args):
        qi, bi = args
        z = jnp.einsum("bhqd,bhkd->bhqk", qi, k, preferred_element_type=jnp.float32) * scale
        qpos = bi * BLOCK_Q + jnp.arange(BLOCK_Q)
        causal = kpos[None, :] < qpos[:, None]
        log_1m_beta = jnp.where(causal, -jax.nn.softplus(z), 0.0)
        rest = lax.cumsum(log_1m_beta, axis=log_1m_beta.ndim - 1, reverse=True) - log_1m_beta
        attn = jnp.where(causal, jnp.exp(jax.nn.log_sigmoid(z) + rest), 0.0)
        return jnp.einsum("bhqk,bhkd->bhqd", attn.astype(v.dtype), v)

    out = lax.map(one_block, (qb, jnp.arange(nb)))
    return out.transpose(1, 2, 0, 3, 4).reshape(b, h, s, dh)

def second_inputs(seed: int = 0) -> dict:
    key = jax.random.key(seed)
    ks = jax.random.split(key, 20)
    f32 = jnp.float32

    def nrm(k, shape, fan_in):
        return jax.random.normal(k, shape, f32) * (fan_in ** -0.5)

    def gain(k, shape):
        return 1.0 + 0.05 * jax.random.normal(k, shape, f32)

    def small(k, shape):
        return 0.02 * jax.random.normal(k, shape, f32)

    L = DEPTH_2
    return {
        "x": jax.random.normal(ks[0], (BATCH, SEQ, D_MODEL), f32),
        "mix_norm_g": gain(ks[1], (L, D_MODEL)),
        "w_in": nrm(ks[2], (L, D_MODEL, N_IN), D_MODEL),
        "q_norm_g": gain(ks[3], (L, HEAD_DIM)),
        "k_norm_g": gain(ks[4], (L, HEAD_DIM)),
        "w_attn_out": nrm(ks[5], (L, W_ATTN, D_MODEL), W_ATTN),
        "conf_dw_w": nrm(ks[6], (L, CONF_WIDTH, C_CONF), CONF_WIDTH),
        "conf_dw_b": small(ks[7], (L, C_CONF)),
        "conf_ln_g": gain(ks[8], (L, C_CONF)),
        "conf_ln_b": small(ks[9], (L, C_CONF)),
        "w_conf_out": nrm(ks[10], (L, C_CONF, D_MODEL), C_CONF),
        "sc_conv_w": nrm(ks[11], (L, SC_WIDTH, C_SC), SC_WIDTH),
        "w_sc_out": nrm(ks[12], (L, C_SC, D_MODEL), C_SC),
        "gate_b": small(ks[13], (L, N_BRANCH, D_MODEL)),
        "w_o": nrm(ks[14], (L, D_MODEL, D_MODEL), D_MODEL),
        "ffn_norm_g": gain(ks[15], (L, D_MODEL)),
        "w_ffn_in": nrm(ks[16], (L, D_MODEL, 2 * D_FF_2), D_MODEL),
        "w_ffn_out": nrm(ks[17], (L, D_FF_2, D_MODEL), D_FF_2),
    }

def second_block(x, mix_norm_g, w_in, q_norm_g, k_norm_g, w_attn_out, conf_dw_w, conf_dw_b,
              conf_ln_g, conf_ln_b, w_conf_out, sc_conv_w, w_sc_out, gate_b, w_o,
              ffn_norm_g, w_ffn_in, w_ffn_out):
    b, s, _ = x.shape
    for l in range(DEPTH_2):
        u = rms_norm(x, mix_norm_g[l])
        proj = u @ w_in[l]
        q, k, v, cf_val, cf_gate, sc_x, sc_bg, sc_cg, gates = jnp.split(proj, SPLIT_IDX, axis=-1)

        q = rms_norm(q.reshape(b, s, N_HEADS, HEAD_DIM), q_norm_g[l]).transpose(0, 2, 1, 3)
        k = rms_norm(k.reshape(b, s, N_HEADS, HEAD_DIM), k_norm_g[l]).transpose(0, 2, 1, 3)
        v = v.reshape(b, s, N_HEADS, HEAD_DIM).transpose(0, 2, 1, 3)
        o = stick_breaking_attention(q, k, v).transpose(0, 2, 1, 3).reshape(b, s, W_ATTN)
        y_a = o @ w_attn_out[l]

        hb = cf_val * jax.nn.sigmoid(cf_gate)
        hb = causal_depthwise_conv(hb, conf_dw_w[l]) + conf_dw_b[l]
        hb = jax.nn.silu(layer_norm(hb, conf_ln_g[l], conf_ln_b[l]))
        y_b = hb @ w_conf_out[l]

        hc = sc_bg * causal_depthwise_conv(sc_cg * sc_x, sc_conv_w[l])
        y_c = hc @ w_sc_out[l]

        g = jax.nn.sigmoid(gates.reshape(b, s, N_BRANCH, D_MODEL) + gate_b[l])
        merged = g[:, :, 0] * y_a + g[:, :, 1] * y_b + g[:, :, 2] * y_c
        x = x + merged @ w_o[l]

        hf = rms_norm(x, ffn_norm_g[l]) @ w_ffn_in[l]
        gt, up = jnp.split(hf, 2, axis=-1)
        x = x + (jax.nn.silu(gt) * up) @ w_ffn_out[l]
    return x


def setup_inputs(seed=0):
    out = dict(first_inputs(seed))
    for name, value in second_inputs(seed + 1).items():
        if name != "x":
            out[name + "_2"] = value
    return out


def reference(
    x, meta_tokens, ffn1_norm, ffn1_w_gate, ffn1_w_up, ffn1_w_down, mix_norm, ffn2_norm,
    ffn2_w_gate, ffn2_w_up, ffn2_w_down, pool_w, pool_scale, kv_in_norm, w_dkv, kv_latent_norm,
    w_uk, w_uv, w_dq, q_latent_norm, w_uq, w_o, final_norm, mix_norm_g_2, w_in_2, q_norm_g_2,
    k_norm_g_2, w_attn_out_2, conf_dw_w_2, conf_dw_b_2, conf_ln_g_2, conf_ln_b_2, w_conf_out_2,
    sc_conv_w_2, w_sc_out_2, gate_b_2, w_o_2, ffn_norm_g_2, w_ffn_in_2, w_ffn_out_2,
):
    x = first_block(
        x, meta_tokens, ffn1_norm, ffn1_w_gate, ffn1_w_up, ffn1_w_down, mix_norm, ffn2_norm,
        ffn2_w_gate, ffn2_w_up, ffn2_w_down, pool_w, pool_scale, kv_in_norm, w_dkv,
        kv_latent_norm, w_uk, w_uv, w_dq, q_latent_norm, w_uq, w_o, final_norm,
    )
    return second_block(
        x, mix_norm_g_2, w_in_2, q_norm_g_2, k_norm_g_2, w_attn_out_2, conf_dw_w_2, conf_dw_b_2,
        conf_ln_g_2, conf_ln_b_2, w_conf_out_2, sc_conv_w_2, w_sc_out_2, gate_b_2, w_o_2,
        ffn_norm_g_2, w_ffn_in_2, w_ffn_out_2,
    )


_drawn_inputs = setup_inputs


def setup_inputs(seed=0):
    import zlib

    import numpy as np

    out = dict(_drawn_inputs(seed))
    spreads = {}
    factors = {'kv_in_norm': 3.573,
     'kv_latent_norm': 3.584,
     'q_latent_norm': 4.994,
     'q_norm_g_2': 7.58,
     'k_norm_g_2': 7.648,
     'conf_dw_b_2': 5.107,
     'conf_ln_g_2': 3.375,
     'conf_ln_b_2': 8.0,
     'gate_b_2': 8.0}
    for name, (base, spread) in spreads.items():
        noise = np.random.default_rng([zlib.crc32(name.encode()), seed]).standard_normal(out[name].shape)
        drawn = base * np.exp(spread * noise) if base else spread * noise
        out[name] = __import__('jax').numpy.asarray(drawn.astype(out[name].dtype))
    for name, factor in factors.items():
        out[name] = (out[name] * factor).astype(out[name].dtype)
    return out
```

```python
from contextlib import ExitStack

import numpy as np

import concourse.bass as bass
from concourse import mybir

F32 = mybir.dt.float32
F32R = mybir.dt.float32r
ALU = mybir.AluOpType
ACT = mybir.ActivationFunctionType
AX_X = mybir.AxisListType.X

P = 128
D = 1024
KD = D // P
SEQ = 512
NT = SEQ // P
NMETA = 16
T1 = SEQ + NMETA
HALF = T1 // 2
FF = 2816
PAIRS = (6, 5)
FMAX = 2 * max(PAIRS)
NH, DN, DR, DV = 8, 64, 32, 64
DQK = DN + DR
RKV, RQ = 256, 384
KKV, KQ = RKV // P, RQ // P
EPS = 1e-6
SM_SCALE = float(1.0 / np.sqrt(DQK))
SEC = {"q": 0, "k": 512, "v": 1024, "cv": 1536, "cg": 2048, "sx": 2560, "sb": 3072, "sc": 3584,
       "gate": 4096}
CW = 512
CT = CW // P
CONV, SCW = 31, 3
RING = 4
UW = 1024
SLOTS = 4
BANK = 512
NEG = -1.0e30
POOL_W = (2, 4, 8, 16)

C_ID, C_NTRI, C_NONE, C_ONE, C_BLK, C_MASK = (i * P for i in range(6))
C_CNT = 6 * P
C_MAIN = C_CNT + 4 * NMETA
TAB_Q, TAB_COS, TAB_SIN = range(3)

G1, G2 = {}, {}


def _rows(table, name, n):
    table[name] = (sum(v[1] for v in table.values()), n)


for _n, _k in (("ffn1_norm", 16), ("mix_norm", 16), ("ffn2_norm", 16), ("pool_scale", 8),
               ("kv_in_norm", 8), ("kv_latent_norm", 2), ("q_latent_norm", 3), ("final_norm", 8)):
    _rows(G1, _n, _k)
for _n, _k in (("mix_norm_g_2", 8), ("q_norm_g_2", 1), ("k_norm_g_2", 1), ("conf_dw_b_2", 4),
               ("conf_ln_g_2", 4), ("conf_ln_b_2", 4), ("sc_conv_w_2", 12), ("gate_b_2", 24),
               ("ffn_norm_g_2", 8)):
    _rows(G2, _n, _k)
N1 = sum(v[1] for v in G1.values())
N2 = sum(v[1] for v in G2.values())
N3 = CONV * CT


class Counts:

    def __init__(self):
        self.value, self.stride, self.slot, self.known = {}, {}, {}, False

    def start(self):
        self.n = {"pe": 0, "dve": 0, "act": 0}
        self.loop = {"pe": None, "dve": None, "act": None}

    def tick(self, eng, *names):
        self.n[eng] += 1
        for name in names:
            assert self.known or (eng, name) not in self.value, name
            self.value[eng, name] = self.n[eng]
            if self.loop[eng]:
                self.loop[eng][2].append(name)

    def at(self, eng, name, i=0):
        if not self.known:
            return 1
        v = self.value[eng, name]
        return v + self.stride[eng, name] * i if (eng, name) in self.stride else v

    def here(self, eng):
        lp = self.loop[eng]
        return self.n[eng] + (lp[0] * lp[1] if lp else 0)

    def enter(self, eng, key, i):
        stride = self.stride.get((eng, "loop:" + key), 1)
        self.loop[eng] = (i, stride, [], self.n[eng], key)

    def leave(self, eng, count):
        _, _, names, first, key = self.loop[eng]
        body = self.n[eng] - first
        self.stride[eng, "loop:" + key] = body
        for name in names:
            self.stride[eng, name] = body
            if eng != "pe":
                assert self.value[eng, name] - body == self.value[eng, name.replace(":L:", ":0:")]
        self.n[eng] = first + body * count
        self.loop[eng] = None


def units():
    out = []

    def ffn(f):
        for part, pairs in enumerate(PAIRS):
            for j in range(4 * pairs):
                out.append((f"gu{f}{part}", j))
            for j in range(2 * pairs):
                out.append((f"dn{f}{part}", j))

    def stage(name, n):
        out.extend((name, j) for j in range(n))

    ffn(0)
    stage("pool", 2)
    ffn(1)
    stage("dkv", 4)
    ffn(2)
    for name, n in (("dq", 3), ("uq", 4), ("uk", 1), ("uv", 1), ("wo", 4)):
        stage(name, n)
    ffn(3)
    for name, n in (("qk", 8), ("v", 4), ("cf", 8), ("sc", 12), ("br", 36), ("wo2", 8)):
        stage(name, n)
    ffn(4)
    return out


UNITS = units()
NUNITS = len(UNITS)
U0 = {}
for _u, (_s, _j) in enumerate(UNITS):
    U0.setdefault(_s, _u)


def unit_dmas(stage, j):
    return {"dkv": 2 * (1 + 4 + 8), "uq": 3 * 4}.get(stage, 1)


RAW_AT = []
_sum = [0] * RING
for _u, (_s, _j) in enumerate(UNITS):
    _sum[_u % RING] += 16 * unit_dmas(_s, _j)
    RAW_AT.append(_sum[_u % RING])


def mla_order():
    steps = [(h, i) for h in range(NH) for i in range(NT + 1)]
    order = []
    for s in range(len(steps) + 4):
        if s < len(steps):
            order.append(("S",) + steps[s])
        if 0 <= s - 3 < len(steps):
            order.append(("T",) + steps[s - 3])
        if 0 <= s - 4 < len(steps) and steps[s - 4][1] == NT:
            order.append(("V", steps[s - 4][0], 0))
    return order


def blend_order():
    quarters = [(st, n, e, f) for st, pairs in (("cf", 4), ("sc", 6)) for n in range(pairs)
                for e in range(2) for f in range(2)]
    after = {"z": 3, "r": 1, "o": 1}
    order = []
    for hd in range(NH):
        for what, n in after.items():
            order.append((what, hd))
            order += quarters[:n]
            del quarters[:n]
    return order + quarters


def program(nc, w, out, consts, tables, C):
    C.start()
    at = C.at
    ctx = ExitStack()
    with ctx:
        def sem(name):
            return ctx.enter_context(nc.semaphore(name))

        top = [nc.sbuf_base if not callable(nc.sbuf_base) else nc.sbuf_base()]
        limit = nc.sbuf_usable_end if not callable(nc.sbuf_usable_end) else nc.sbuf_usable_end()

        def place(name, shape, dt=F32, at=None):
            size = int(np.prod(shape[1:])) * 4
            size = (size + 31) // 32 * 32
            if at is None:
                at = top[0]
                top[0] += size
                assert top[0] <= limit, (name, top[0], limit)
            return nc.alloc_sbuf_tensor_at(name, list(shape), dt, offset=at)

        def zone(size):
            at = top[0]
            top[0] += (size + 31) // 32 * 32
            assert top[0] <= limit, (size, top[0], limit)
            return at

        top[0] = (top[0] + 31) // 32 * 32
        raw = place("raw", [P, RING, UW])
        wH = place("wH", [P, RING, UW], F32R)
        wL = place("wL", [P, RING, UW], F32R)
        h = place("h", [P, KD, T1])
        x2 = h[:, :, NMETA:T1]
        cst = place("cst", [P, C_MAIN])
        g1 = place("g1", [P, N1])
        g2 = place("g2", [P, N2])
        g3 = place("g3", [P, N3])
        rs = place("rs", [P, T1])
        rl = place("rl", [P, T1])
        hbn_at = top[0]
        var = place("var", [P, T1])
        ss = place("ss", [P, T1])
        sd = place("sd", [P, T1])
        z1 = top[0]
        t1 = place("t1", [P, 2, T1])
        t2 = place("t2", [P, 2, T1])
        m = place("m", [P, 2, T1])
        sq = place("sq", [P, 2, T1])
        small = place("small", [P, 16])
        zx = zone(KD * T1 * 8)
        xH = place("xH", [P, KD, T1], F32R, zx)
        xL = place("xL", [P, KD, T1], F32R, zx + KD * T1 * 4)
        za = zone(FMAX * T1 * 8)
        aH = place("aH", [P, FMAX, T1], F32R, za)
        aL = place("aL", [P, FMAX, T1], F32R, za + FMAX * T1 * 4)
        zs = zone(KD * SEQ * 4)
        clat = place("clat", [P, KKV, T1], F32, zs)
        krope = place("krope", [P, T1], F32, zs + KKV * T1 * 4)
        tab = place("tab", [P, 3, T1], F32, zs + 3 * T1 * 4)
        xin = place("xin", [P, NT, D], F32, za)
        metain = place("metain", [P, D], F32, za + NT * D * 4)
        grow = place("grow", [P, 3, P], F32, za + (NT + 1) * D * 4)
        yout = place("yout", [P, 2, D], F32, za)
        cqH = place("cqH", [P, KQ, T1], F32R, za)
        cqL = place("cqL", [P, KQ, T1], F32R, za + KQ * T1 * 4)
        oH = place("oH", [P, NH // 2, T1], F32R, za)
        oL = place("oL", [P, NH // 2, T1], F32R, za + NH // 2 * T1 * 4)
        zq = za + NH * T1 * 4
        qcat = place("qcat", [P, NH, T1], F32, zq)
        zv = zq + NH * T1 * 4
        vreal = place("vreal", [P, NT, NH * DV], F32, zv)
        vmeta = place("vmeta", [P, NH * DV], F32, zv + NT * NH * DV * 4)
        pmT = place("pmT", [P, T1], F32, zv + (NT + 1) * NH * DV * 4)
        cqr = place("cqr", [P, KQ, T1], F32, zq)
        cnH = place("cnH", [P, KKV, T1], F32R, zx)
        cnL = place("cnL", [P, KKV, T1], F32R, zx + KKV * T1 * 4)
        kcat = place("kcat", [P, NH, T1], F32, zx + 2 * KKV * T1 * 4)
        pT = place("pT", [P, NT, SEQ], F32, zx + (2 * KKV + NH) * T1 * 4)
        prob = place("prob", [P, 4, T1], F32, z1 + 4 * T1 * 4)
        hbw = CONV - 1 + SEQ
        scw = SCW - 1 + SEQ
        zc = za + 2 * CT * SEQ * 4
        zk = zc + 2 * CT * SEQ * 4
        hb = place("hb", [P, CT, hbw], F32, za)
        xc = place("xc", [P, 2, scw], F32, z1 + 6 * T1 * 4)
        tri = [sum(SEQ - i * P for i in range(j)) for j in range(NT + 1)]
        spls = place("spls", [P, tri[NT]], F32, za + CT * hbw * 4)
        assert CT * hbw + tri[NT] <= 2 * CT * SEQ
        v2 = place("v2", [P, NT, CW], F32, zs)
        qpad = place("qpad", [P, SEQ], F32, zs + NT * CW * 4)
        attns = place("attns", [P, tri[NT]], F32, zs + (NT * CW + SEQ) * 4)
        conv = place("conv", [P, CT, SEQ], F32, zc)
        hcr = place("hcr", [P, CT, SEQ], F32, zc + CT * SEQ * 4)
        q2 = place("q2", [P, CT, SEQ], F32, zk)
        k2 = place("k2", [P, CT, SEQ], F32, zk + CT * SEQ * 4)
        o2 = q2
        o2L = place("o2L", [P, CT, SEQ], F32R, zk)
        o2H = place("o2H", [P, CT, SEQ], F32R, zk + CT * SEQ * 4)
        hbH = place("hbH", [P, CT, SEQ], F32R, za)
        hbL = place("hbL", [P, CT, SEQ], F32R, za + CT * SEQ * 4)
        hcH = place("hcH", [P, CT, SEQ], F32R, zc)
        hcL = place("hcL", [P, CT, SEQ], F32R, zc + CT * SEQ * 4)
        hbn = place("hbn", [P, 2, T1], F32, hbn_at)
        lnt = sq
        merged = place("merged", [P, KD, SEQ], F32, zs)
        mgH = place("mgH", [P, KD, SEQ], F32R, za)
        mgL = place("mgL", [P, KD, SEQ], F32R, zk)
        PAD = max(POOL_W) // 2
        zpad = place("zpad", [P, PAD + T1], F32, zs)
        wpad = place("wpad", [P, 2, PAD + T1], F32, z1)

        def spl(j):
            return spls[:, tri[j]:tri[j + 1]]

        def attn(j):
            return attns[:, tri[j]:tri[j + 1]]

        ps = ctx.enter_context(nc.psum_tensor("ps", [P, 2 * SLOTS, BANK], F32))
        ident = cst[:, C_ID:C_ID + P]
        ntri = cst[:, C_NTRI:C_NTRI + P]
        none_ = cst[:, C_NONE:C_NONE + P]
        ones = cst[:, C_ONE:C_ONE + P]
        blk = cst[:, C_BLK:C_BLK + P]
        mask = cst[:, C_MASK:C_MASK + P]

        def pairs(ap):
            return ap.rearrange("p (c n) -> p c n", c=2)

        def slot(name, T):
            s = C.slot.get(name, 0)
            return ps[:, 2 * s:2 * s + 2, 0:HALF] if T == T1 else ps[:, 2 * s, 0:T]

        def like(ap, T):
            return pairs(ap) if T == T1 else ap

        def flat(s):
            return ps[:, 2 * s:2 * s + 2, :].rearrange("p c n -> p (c n)")

        def f32(ap):
            return ap.bitcast(F32)

        def gcol(table, name, k):
            t, rows = (g1, G1) if table == 1 else (g2, G2)
            if name.endswith("norm1"):
                name, k = name[:-1], k + KD
            return t[:, rows[name][0] + k:rows[name][0] + k + 1]

        raw_in = [sem(f"raw_in{s}") for s in range(RING)]
        h_done = sem("hi_done")
        l_done = sem("lo_done")
        pe_done = sem("pe_done")
        dve_done = sem("dve_done")
        act_done = sem("act_done")
        s_x = sem("x_in")
        s_c = sem("consts_in")
        s_g = sem("gains_in")
        s_t = sem("tables_in")
        s_out = [sem(f"out_done{s}") for s in range(2)]

        block = ctx.enter_context(nc.Block())

        def ffn_weights(f):
            if f < 4:
                a, l = ("ffn1", "ffn2")[f % 2], f // 2
                return w[a + "_w_gate"][l], w[a + "_w_up"][l], w[a + "_w_down"][l]
            wi = w["w_ffn_in_2"][0]
            return wi[:, 0:FF], wi[:, FF:2 * FF], w["w_ffn_out_2"][0]

        def ftok(f):
            return T1 if f < 4 else SEQ

        @block.sync
        def _(sp):
            sp.dma_start(xin[:, :, :], w["x"][0].rearrange("(t p) d -> p t d", p=P)).then_inc(s_x, 16)
            sp.dma_start(metain[0:NMETA, :], w["meta_tokens"]).then_inc(s_x, 16)
            sp.dma_start(cst[:, :], consts).then_inc(s_c, 16)
            n = 0
            for tabn, rows in ((0, G1), (1, G2)):
                for name, (r, k) in rows.items():
                    if name in ("q_norm_g_2", "k_norm_g_2"):
                        for half in range(2):
                            sp.dma_start(grow[r:r + 1, tabn, half * DV:(half + 1) * DV], w[name])\
                                .then_inc(s_g, 16)
                            n += 1
                        continue
                    src = w[name]
                    if name == "sc_conv_w_2":
                        src = src.rearrange("l s (k p) -> (l s k) p", p=P)
                    elif name == "gate_b_2":
                        src = src.rearrange("l b (k p) -> (l b k) p", p=P)
                    elif len(src.shape) == 1:
                        src = src.rearrange("(k p) -> k p", p=P)
                    else:
                        src = src.rearrange("l (k p) -> (l k) p", p=P)
                    sp.dma_start(grow[r:r + k, tabn, :], src).then_inc(s_g, 16)
                    n += 1
            sp.dma_start(grow[0:N3, 2, :], w["conf_dw_w_2"].rearrange("l s (k p) -> (l s k) p", p=P))\
                .then_inc(s_g, 16)
            C.gain_dmas = n + 1
            sp.dma_start(tab[:, :, :], tables).then_inc(s_t, 16)

            def load(u, src, i=0):
                if u >= RING or not isinstance(i, int):
                    sp.wait_ge(l_done, u - RING + 1 + RING * i)
                n = src.shape[1] * src.shape[2]
                sp.dma_start(raw[:, u % RING, 0:n].rearrange("p (a b) -> p a b", a=src.shape[1]),
                             src).then_inc(raw_in[u % RING], 16)

            def kpart(wt, k0, nk, c0, c1):
                return wt[k0 * P:(k0 + nk) * P, c0:c1].rearrange("(a p) c -> p a c", p=P)

            def load_ffn(f):
                gate, up, down = ffn_weights(f)
                row = 0
                for part, n in enumerate(PAIRS):
                    u = U0[f"gu{f}{part}"]

                    def gu(i, c):
                        for j in range(4):
                            wt = (gate, gate, up, up)[j]
                            src = wt[(j % 2) * 4 * P:(j % 2 + 1) * 4 * P, bass.ds(c, 2 * P)]
                            load(u + j, src.rearrange("(a p) c -> p a c", p=P), i)

                    gu(0, row * P)
                    with sp.Fori(1, n) as i:
                        gu(i, row * P + i * (2 * P))
                    u = U0[f"dn{f}{part}"]
                    for dg in range(2):
                        for j in range(n):
                            load(u + dg * n + j, kpart(down, row + 2 * j, 2, dg * BANK, (dg + 1) * BANK))
                    row += 2 * n

            load_ffn(0)
            for j in range(2):
                load(U0["pool"] + j,
                     w["pool_w"][0, 2 * j:2 * j + 2].rearrange("g (a p) d -> p (g a) d", p=P))
            load_ffn(1)
            for j in range(4):
                u = U0["dkv"] + j
                sp.wait_ge(l_done, u - RING + 1)
                for a in range(2):
                    kt = w["w_dkv"][(2 * j + a) * P:(2 * j + a + 1) * P, :]
                    dst = raw[:, u % RING, a * 512:(a + 1) * 512]
                    sp.dma_start(dst[:, 0:RKV], kt[:, 0:RKV]).then_inc(raw_in[u % RING], 16)
                    for r in range(4):
                        o = RKV + r * DR
                        sp.dma_start(dst[:, o:o + DR], kt[:, RKV:RKV + DR])\
                            .then_inc(raw_in[u % RING], 16)
                        for e in range(2):
                            o = RKV + P + r * DR + e * (DR // 2)
                            f0 = RKV + (1 - e) * (DR // 2)
                            sp.dma_start(dst[:, o:o + DR // 2], kt[:, f0:f0 + DR // 2])\
                                .then_inc(raw_in[u % RING], 16)
            load_ffn(2)
            for j in range(3):
                load(U0["dq"] + j, kpart(w["w_dq"][0], 0, KD, j * P, (j + 1) * P))
            for j in range(4):
                u = U0["uq"] + j
                sp.wait_ge(l_done, u - RING + 1)
                for a in range(KQ):
                    kt = w["w_uq"][0, a * P:(a + 1) * P, 2 * j * DQK:(2 * j + 2) * DQK]\
                        .rearrange("p (e c) -> p e c", e=2)
                    dst = raw[:, u % RING, a * 2 * P:(a + 1) * 2 * P].rearrange("p (e c) -> p e c", e=2)
                    for o, f0, n in ((0, 0, DN), (DN, DN, DR), (DQK, DN + DR // 2, DR // 2),
                                     (DQK + DR // 2, DN, DR // 2)):
                        sp.dma_start(dst[:, :, o:o + n], kt[:, :, f0:f0 + n])\
                            .then_inc(raw_in[u % RING], 16)
            load(U0["uk"], kpart(w["w_uk"], 0, KKV, 0, NH * DN))
            load(U0["uv"], kpart(w["w_uv"], 0, KKV, 0, NH * DV))
            for j in range(4):
                load(U0["wo"] + j, kpart(w["w_o"][0], 0, 4, 2 * j * P, 2 * (j + 1) * P))
            load_ffn(3)
            win = w["w_in_2"][0]

            def load_pair(u, c):
                for e in range(2):
                    load(u + e, kpart(win, 4 * e, 4, c, c + 2 * P))

            for e in range(4):
                load_pair(U0["qk"] + 2 * e, SEC["qk"[e // 2]] + 2 * (e % 2) * P)
            for j in range(4):
                load(U0["v"] + j, kpart(win, 2 * j, 2, SEC["v"], SEC["v"] + CW))
            for p in range(2):
                for e, s in enumerate(("cv", "cg")):
                    load_pair(U0["cf"] + 4 * p + 2 * e, SEC[s] + 2 * p * P)
            for p in range(2):
                for e, s in enumerate(("sx", "sc", "sb")):
                    load_pair(U0["sc"] + 6 * p + 2 * e, SEC[s] + 2 * p * P)
            for b, name in enumerate(("w_attn_out_2", "w_conf_out_2", "w_sc_out_2")):
                for p in range(4):
                    u = U0["br"] + (b * 4 + p) * 3
                    load(u, kpart(w[name][0], 0, CT, 2 * p * P, 2 * (p + 1) * P))
                    load_pair(u + 1, SEC["gate"] + b * D + 2 * p * P)
            for p in range(4):
                for e in range(2):
                    load(U0["wo2"] + 2 * p + e, kpart(w["w_o_2"][0], 4 * e, 4, 2 * p * P, 2 * (p + 1) * P))
            load_ffn(4)
            for t in range(NT):
                sp.wait_ge(dve_done, at("dve", f"yout{t}"))
                sp.dma_start(out[0, t * P:(t + 1) * P, :], yout[:, t % 2, :]).then_inc(s_out[t % 2], 16)
            for s in s_out:
                sp.wait_ge(s, 16 * NT // 2)

        @block.gpsimd
        def _(pool):
            def lo(u, i=0):
                s = u % RING
                pool.wait_ge(h_done, u + 1 + RING * i)
                nc.gpsimd.tensor_tensor(wL[:, s, :], raw[:, s, :], f32(wH[:, s, :]),
                                        ALU.subtract).then_inc(l_done, 1)

            with pool.Fori(0, NUNITS // RING) as i:
                for s in range(RING):
                    lo(s, i)
            for u in range(NUNITS // RING * RING, NUNITS):
                lo(u)

        @block.tensor
        def _(pe):
            owner = [None] * SLOTS
            count = [0]

            def done(ins, name):
                ins.then_inc(pe_done, 1)
                C.tick("pe", name)

            def group(name, reader=None):
                s = count[0] % SLOTS
                count[0] += 1
                if owner[s]:
                    eng, ev, i = owner[s]
                    pe.wait_ge({"dve": dve_done, "act": act_done}[eng], at(eng, ev, i))
                owner[s] = reader or ("dve", "rd:" + name, 0)
                C.slot[name] = s
                return s

            def product(s, T, wcol, sl, rhs, start, stop):
                aH_, aL_ = rhs
                parts = [(0, HALF), (HALF, T1)] if T == T1 else [(0, T)]
                wh, wl = wH[:, sl, wcol:wcol + P], wL[:, sl, wcol:wcol + P]
                for n, (lhs, r) in enumerate(((wh, aH_), (wh, aL_), (wl, aH_))):
                    for c, (a, b) in enumerate(parts):
                        ins = nc.tensor.matmul(ps[:, 2 * s + c, 0:b - a], lhs, r[:, a:b],
                                               start=start and n == 0, stop=stop and n == 2,
                                               skip_group_check=True)
                return ins

            def weights(u, i=0):
                pe.wait_ge(l_done, u + 1 + RING * i)

            def xs(k, T):
                return xH[:, k, 0:T], xL[:, k, 0:T]

            def stats(name, s, src, lhs, ev):
                pe.wait_ge(dve_done, at("dve", ev))
                for n, ap in enumerate(src):
                    T = ap.shape[1]
                    cuts = [(0, HALF), (HALF, T1)] if T == T1 else [(0, T)]
                    for c, (a, b) in enumerate(cuts):
                        ins = nc.tensor.matmul(ps[:, 2 * s + c, 0:b - a], lhs, ap[:, a:b],
                                               start=n == 0, stop=n == len(src) - 1,
                                               skip_group_check=True)
                done(ins, name)

            def norm_stats(p, T, s):
                stats(f"st:{p}", s, [ss[:, 0:T]], ones, f"ss:{p}:{KD - 1}")

            def borrow(p, T, ahead):
                s = (count[0] + ahead) % SLOTS
                if owner[s]:
                    eng, ev, i = owner[s]
                    pe.wait_ge({"dve": dve_done, "act": act_done}[eng], at(eng, ev, i))
                norm_stats(p, T, s)
                owner[s] = ("dve", f"rd:st:{p}", 0)
                C.slot[f"st:{p}"] = s

            def ffn(f):
                T = ftok(f)
                for part, n in enumerate(PAIRS):
                    st = f"gu{f}{part}"
                    u = U0[st]

                    def gu(it, i, first):
                        for half, what in enumerate(("gate", "up")):
                            sl = []
                            for j in range(2):
                                name = f"{st}:{it}:{what}{j}"
                                s = count[0] % SLOTS
                                if it == "L":
                                    pe.wait_ge(dve_done, at("dve", "rd:" + name, i - 2))
                                    count[0] += 1
                                    C.slot[name] = s
                                    owner[s] = ("dve", "rd:" + name, n - 2)
                                    sl.append(s)
                                elif half == 1 and j == 1 and first:
                                    sl.append(None)
                                else:
                                    sl.append(group(name))
                            for e in range(2):
                                uu = u + 2 * half + e
                                weights(uu, i)
                                for j in range(2):
                                    name = f"{st}:{it}:{what}{j}"
                                    if sl[j] is None:
                                        sl[j] = group(name)
                                    for k in range(4):
                                        if first and half == 0 and j == 0:
                                            pe.wait_ge(dve_done, at("dve", f"xl:f{f}:{4 * e + k}"))
                                        ins = product(sl[j], T, k * 2 * P + j * P, uu % RING,
                                                      xs(4 * e + k, T), e == 0 and k == 0,
                                                      e == 1 and k == 3)
                                    if e == 1 and j == 0:
                                        done(ins, name)
                                done(ins, f"{st}:{it}:u{2 * half + e}" if e == 0 else
                                     f"{st}:{it}:{what}1")
                            if first and half == 0 and f != 2:
                                borrow(f"f{f}", T, 1)

                    gu("0", 0, part == 0)
                    with pe.Fori(1, n) as i:
                        C.enter("pe", st, i - 1)
                        gu("L", i, False)
                        C.leave("pe", n - 1)
                    st = f"dn{f}{part}"
                    u = U0[st]
                    for dg in range(2):
                        sl = [group(f"{st}:{4 * dg + d}") for d in range(4)]
                        for j in range(n):
                            weights(u + dg * n + j)
                            for d in range(4):
                                for e in range(2):
                                    if dg == 0 and d == 0:
                                        it = ("0", 0) if j == 0 else ("L", j - 1)
                                        pe.wait_ge(dve_done, at("dve", f"gu{f}{part}:{it[0]}:lo{e}", it[1]))
                                    fl = 2 * j + e
                                    ins = product(sl[d], T, e * 512 + d * P, (u + dg * n + j) % RING,
                                                  (aH[:, fl, 0:T], aL[:, fl, 0:T]),
                                                  fl == 0, fl == 2 * n - 1)
                                if j == n - 1 and d < 3:
                                    done(ins, f"{st}:{4 * dg + d}")
                            done(ins, f"{st}:{4 * dg + 3}" if j == n - 1 else f"{st}:u{dg * n + j}")

            def transposed(dst, src, n):
                return nc.tensor.transpose(dst, src, ident[0:n, 0:n])

            pe.wait_ge(s_c, 16)
            pe.wait_ge(s_g, 16 * C.gain_dmas)
            for n, rows in enumerate((N1, N2, N3)):
                s = group(f"g{n}")
                done(transposed(ps[:, 2 * s, 0:rows], grow[0:rows, n, :], rows), f"g{n}")
            pe.wait_ge(s_x, 32)
            for k in range(KD):
                s = group(f"in{k}")
                transposed(ps[:, 2 * s + 1, 0:NMETA], metain[0:NMETA, k * P:(k + 1) * P], NMETA)
                for t in range(NT):
                    ins = transposed(ps[:, 2 * s, t * P:(t + 1) * P], xin[:, t, k * P:(k + 1) * P], P)
                done(ins, f"in{k}")

            ffn(0)

            norm_stats("pool", T1, group("st:pool"))
            for j in range(2):
                weights(U0["pool"] + j)
                for d in range(4):
                    s = group(f"pool:{4 * j + d}")
                    g = 2 * j + d // 2
                    for a in range(2):
                        k = 2 * g + a
                        pe.wait_ge(dve_done, at("dve", f"xl:pool:{k}"))
                        ins = product(s, T1, (d // 2 * 2 + a) * 2 * P + d % 2 * P,
                                      (U0["pool"] + j) % RING, xs(k, T1), a == 0, a == 1)
                    done(ins, f"pool:{4 * j + d}")

            ffn(1)

            norm_stats("dkv", T1, group("st:dkv"))
            sl = [group(f"dkv:{d}") for d in range(4)]
            for j in range(4):
                weights(U0["dkv"] + j)
                for d in range(4):
                    for a in range(2):
                        k = 2 * j + a
                        if d == 0:
                            pe.wait_ge(dve_done, at("dve", f"xl:dkv:{k}"))
                        ins = product(sl[d], T1, a * 512 + d * P, (U0["dkv"] + j) % RING, xs(k, T1),
                                      k == 0, k == KD - 1)
                    if j == 3:
                        done(ins, f"dkv:{d}")
                if j < 3:
                    done(ins, f"dkv:u{j}")

            ffn(2)

            for j in range(3):
                s = group(f"dq:{j}")
                weights(U0["dq"] + j)
                for k in range(KD):
                    if j == 0:
                        pe.wait_ge(dve_done, at("dve", f"xl:dq:{k}"))
                    ins = product(s, T1, k * P, (U0["dq"] + j) % RING, xs(k, T1), k == 0, k == KD - 1)
                done(ins, f"dq:{j}")
                if j == 1:
                    borrow("dq", T1, 1)
            s = group("st:kv")
            stats("st:kv", s, [ss[:, :]], ones, f"ss:kv:{KKV - 1}")
            s = group("st:cq")
            stats("st:cq", s, [ss[:, :]], ones, f"ss:cq:{KQ - 1}")
            for j in range(4):
                weights(U0["uq"] + j)
                for e in range(2):
                    s = group(f"uq:{2 * j + e}")
                    for k in range(KQ):
                        if j == 0 and e == 0:
                            pe.wait_ge(dve_done, at("dve", f"cql:{k}"))
                        ins = product(s, T1, k * 2 * P + e * P, (U0["uq"] + j) % RING,
                                      (cqH[:, k, :], cqL[:, k, :]), k == 0, k == KQ - 1)
                    done(ins, f"uq:{2 * j + e}")
            weights(U0["uk"])
            for d in range(4):
                s = group(f"uk:{d}", ("act", f"kcat{2 * d + 1}", 0))
                for k in range(KKV):
                    if d == 0:
                        pe.wait_ge(dve_done, at("dve", f"cnl:{k}"))
                    ins = product(s, T1, k * 512 + d * P, U0["uk"] % RING,
                                  (cnH[:, k, :], cnL[:, k, :]), k == 0, k == KKV - 1)
                done(ins, f"uk:{d}")
            weights(U0["uv"])
            for t in range(NT + 1):
                s = group(f"uv:{t}")
                a = NMETA + t * P if t < NT else 0
                sl_ = U0["uv"] % RING
                for k in range(KKV):
                    wh, wl = (x[:, sl_, k * 512:(k + 1) * 512] for x in (wH, wL))
                    ch, cl = (x[:, k, a:a + P] for x in (cnH, cnL))
                    for n, (lhs, r) in enumerate(((ch, wh), (ch, wl), (cl, wh))):
                        ins = nc.tensor.matmul(ps[:, 2 * s, :], lhs, r, start=k == 0 and n == 0,
                                               stop=k == KKV - 1 and n == 2, skip_group_check=True)
                done(ins, f"uv:{t}")

            for what, hd, i in mla_order():
                s = group(f"mla:{what}{hd}:{i}")
                b0, b1 = ps[:, 2 * s, :], ps[:, 2 * s + 1, :]
                if what == "S":
                    pe.wait_ge(act_done, at("act", f"kcat{hd}"))
                    pe.wait_ge(dve_done, at("dve", f"qcat{hd}"))
                    if i < NT:
                        q = qcat[:, hd, NMETA + i * P:NMETA + (i + 1) * P]
                        nc.tensor.matmul(b1[:, 0:NMETA], q, kcat[:, hd, 0:NMETA], start=True, stop=True)
                        ins = nc.tensor.matmul(b0[:, BANK - (i + 1) * P:BANK], q,
                                               kcat[:, hd, NMETA:NMETA + (i + 1) * P],
                                               start=True, stop=True)
                    else:
                        ins = nc.tensor.matmul(b1[0:NMETA, 0:NMETA], qcat[:, hd, 0:NMETA],
                                               kcat[:, hd, 0:NMETA], start=True, stop=True)
                elif what == "T":
                    pe.wait_ge(dve_done, at("dve", f"mla:p{hd}:{i}"))
                    sp_ = (hd * (NT + 1) + i) % 4
                    if i < NT:
                        w0 = BANK - (i + 1) * P
                        for j in range(i + 1):
                            transposed(b0[:, j * P:(j + 1) * P], prob[:, sp_, w0 + j * P:w0 + (j + 1) * P], P)
                        ins = transposed(b1[0:NMETA, 0:P], prob[:, sp_, BANK:BANK + NMETA], P)
                    else:
                        ins = transposed(b1[0:NMETA, 0:NMETA], prob[0:NMETA, sp_, BANK:BANK + NMETA], NMETA)
                else:
                    d = hd // 2
                    pe.wait_ge(dve_done, at("dve", f"rd:mla:T{hd}:{NT}"))
                    cols = slice(d * P, (d + 1) * P)
                    for j in range(NT):
                        nc.tensor.matmul(b0[:, j * P:], vreal[:, j, cols], pT[:, j, j * P:],
                                         start=j == 0, stop=False, skip_group_check=True)
                    nc.tensor.matmul(b0[:, :], vmeta[:, cols], pmT[:, NMETA:], start=False, stop=True,
                                     skip_group_check=True)
                    ins = nc.tensor.matmul(b1[:, 0:NMETA], vmeta[:, cols], pmT[:, 0:NMETA],
                                           start=True, stop=True)
                done(ins, f"mla:{what}{hd}:{i}")

            for j in range(4):
                weights(U0["wo"] + j)
                for e in range(2):
                    s = group(f"wo:{2 * j + e}")
                    for k in range(NH // 2):
                        if j == 0 and e == 0:
                            pe.wait_ge(dve_done, at("dve", f"ol{2 * k}"))
                            pe.wait_ge(dve_done, at("dve", f"ol{2 * k + 1}"))
                        ins = product(s, T1, k * 2 * P + e * P, (U0["wo"] + j) % RING,
                                      (oH[:, k, :], oL[:, k, :]), k == 0, k == NH // 2 - 1)
                    done(ins, f"wo:{2 * j + e}")

            ffn(3)
            norm_stats("final", T1, group("st:final"))

            def quarter(u, stage, n, e, f, kwait=None):
                if e == 0:
                    group(f"{stage}:{2 * n + f}")
                if f == 0:
                    weights(u + e)
                s = C.slot[f"{stage}:{2 * n + f}"]
                for k in range(4):
                    if kwait and f == 0:
                        pe.wait_ge(dve_done, at("dve", f"xl:{kwait}:{4 * e + k}"))
                    ins = product(s, SEQ, k * 2 * P + f * P, (u + e) % RING, xs(4 * e + k, SEQ),
                                  e == 0 and k == 0, e == 1 and k == 3)
                if e == 1:
                    done(ins, f"{stage}:{2 * n + f}")
                elif f == 1:
                    done(ins, f"{stage}:u{u}")

            def mpair(u, stage, n, kwait=None):
                for e in range(2):
                    for f in range(2):
                        quarter(u, stage, n, e, f, kwait)

            def head_stats(n):
                for f in range(2 * n, 2 * n + 2):
                    s = group(f"st:qk:{f}")
                    pe.wait_ge(act_done, at("act", f"sq:qk:{f}"))
                    done(nc.tensor.matmul(ps[:, 2 * s, :], blk, sq[:, f % 2, 0:SEQ], start=True,
                                          stop=True), f"st:qk:{f}")

            for n in range(4):
                mpair(U0["qk"] + 2 * n, "qk", n, "b2" if n == 0 else None)
                if n == 0:
                    borrow("b2", SEQ, 0)
                else:
                    head_stats(n - 1)
            head_stats(3)
            s = group("rcol")
            for t in range(NT):
                ins = nc.tensor.matmul(ps[:, 2 * s, t:t + 1], rs[0:1, t * P:(t + 1) * P],
                                       ones[0:1, 0:1], start=t == 0, stop=t == NT - 1,
                                       skip_group_check=True)
            done(ins, "rcol")
            sl = [group(f"v:{t}") for t in range(NT)]
            for j in range(4):
                weights(U0["v"] + j)
                for t in range(NT):
                    for a in range(2):
                        k = 2 * j + a
                        wh, wl = (x[:, (U0["v"] + j) % RING, a * 512:(a + 1) * 512] for x in (wH, wL))
                        ch, cl = (x[:, k, t * P:(t + 1) * P] for x in (xH, xL))
                        for n, (lhs, r) in enumerate(((ch, wh), (ch, wl), (cl, wh))):
                            ins = nc.tensor.matmul(ps[:, 2 * sl[t], :], lhs, r, start=k == 0 and n == 0,
                                                   stop=k == KD - 1 and n == 2, skip_group_check=True)
                    if j == 3:
                        done(ins, f"v:{t}")
                if j < 3:
                    done(ins, f"v:u{j}")

            def logits(hd):
                pe.wait_ge(act_done, at("act", f"qpad{hd}"))
                if hd:
                    pe.wait_ge(dve_done, at("dve", f"rd:o2:{hd - 1}"))
                for j in reversed(range(NT)):
                    b = ps[:, 2 * j + 1, :]
                    n = SEQ - j * P
                    nc.tensor.matmul(b[:, 0:n], k2[:, hd // 2, j * P:(j + 1) * P], qpad[:, j * P:],
                                     start=True, stop=False, skip_group_check=True)
                    done(nc.tensor.matmul(b[:, 0:P], ident, mask, start=False, stop=False,
                                          skip_group_check=True), f"z{hd}:{j}")

            def sums(hd):
                for j in reversed(range(NT)):
                    b = ps[:, 2 * j + 1, :]
                    pe.wait_ge(dve_done, at("dve", f"sp{hd}:{j}"))
                    for jj in range(j, NT):
                        o = (jj - j) * P
                        ins = nc.tensor.matmul(b[:, o:SEQ - j * P], ntri if jj == j else none_, spl(jj),
                                               start=False, stop=jj == NT - 1, skip_group_check=True)
                    done(ins, f"r{hd}:{j}")

            def values(hd):
                b = ps[:, 2 * NT - 1, :]
                for j in reversed(range(NT)):
                    pe.wait_ge(act_done, at("act", f"a{hd}:{j}"))
                    ins = nc.tensor.matmul(b[:, j * P:], v2[:, j, hd // 2 * P:(hd // 2 + 1) * P], attn(j),
                                           start=j == NT - 1, stop=j == 0, skip_group_check=True)
                done(ins, f"o2:{hd}")

            for what, *at_ in blend_order():
                if what == "z":
                    logits(*at_)
                elif what == "r":
                    sums(*at_)
                elif what == "o":
                    values(*at_)
                else:
                    n, e, f = at_
                    quarter(U0[what] + 2 * n, what, n, e, f)

            inner = ((o2H, o2L), (hbH, hbL), (hcH, hcL))
            ready = ("o2l", "hbl", "hcl")
            for b in range(3):
                for p in range(4):
                    u = U0["br"] + (b * 4 + p) * 3
                    weights(u)
                    for e in range(2):
                        s = group(f"y{b}:{2 * p + e}")
                        for k in range(CT):
                            if p == 0 and e == 0:
                                pe.wait_ge(dve_done, at("dve", f"{ready[b]}{k}"))
                            ins = product(s, SEQ, k * 2 * P + e * P, u % RING,
                                          (inner[b][0][:, k, :], inner[b][1][:, k, :]),
                                          k == 0, k == CT - 1)
                        done(ins, f"y{b}:{2 * p + e}")
                    mpair(u + 1, f"gate{b}", p)
                    if b == 0 and p == 1:
                        stats("st:mean", group("st:mean"), [conv[:, c, :] for c in range(CT)], ones, "conv")
                    if b == 0 and p == 2:
                        stats("st:lnv", group("st:lnv"), [ss[:, 0:SEQ]], ones, f"ss:ln:{CT - 1}")
            for p in range(4):
                u = U0["wo2"] + 2 * p
                sl = [group(f"wo2:{2 * p}"), group(f"wo2:{2 * p + 1}")]
                for e in range(2):
                    weights(u + e)
                    for f in range(2):
                        for k in range(4):
                            if p == 0 and f == 0:
                                pe.wait_ge(dve_done, at("dve", f"mgl{4 * e + k}"))
                            ins = product(sl[f], SEQ, k * 2 * P + f * P, (u + e) % RING,
                                          (mgH[:, 4 * e + k, :], mgL[:, 4 * e + k, :]),
                                          e == 0 and k == 0, e == 1 and k == 3)
                        if e == 1 and f == 0:
                            done(ins, f"wo2:{2 * p}")
                    done(ins, f"wo2:{2 * p + 1}" if e else f"wo2:u{u}")
            ffn(4)
            for t in range(NT):
                s = group(f"out{t}")
                for k in range(KD):
                    pe.wait_ge(dve_done, at("dve", f"h:f4out:{k}"))
                    ins = transposed(ps[:, 2 * s + k // 4, k % 4 * P:(k % 4 + 1) * P],
                                     x2[:, k, t * P:(t + 1) * P], P)
                done(ins, f"out{t}")

        @block.scalar
        def _(act):
            def fn(ins, *names):
                ins.then_inc(act_done, 1)
                C.tick("act", *names)

            def on_dve(name, i=0):
                act.wait_ge(dve_done, at("dve", name, i))

            def on_pe(name, i=0):
                act.wait_ge(pe_done, at("pe", name, i))

            def split(u, i=0, name=None, ix=0):
                if u >= NUNITS:
                    return
                if name:
                    on_pe(name, ix)
                act.wait_ge(raw_in[u % RING], RAW_AT[u] + 16 * i)
                nc.scalar.activation(wH[:, u % RING, :], raw[:, u % RING, :], ACT.Copy)\
                    .then_inc(h_done, 1)

            def after(stage, j, name):
                split(U0[stage] + j + RING, 0, name)

            def src(p, k):
                return x2[:, k, :] if p in ("b2", "f4") else h[:, k, :]

            def prep(p, k, gain, T, squares=True):
                on_dve(f"h:{p}:{k}")
                if squares:
                    if k >= 2:
                        on_dve(f"ss:{p}:{k - 2}")
                    fn(nc.scalar.activation(sq[:, k % 2, 0:T], src(p, k), ACT.Square), f"sq:{p}:{k}")
                if gain:
                    fn(nc.scalar.activation(xH[:, k, 0:T], src(p, k), ACT.Copy, scale=gcol(*gain, k)),
                       f"xh:{p}:{k}")

            def root(p, T):
                on_dve(f"rd:st:{p}")
                fn(nc.scalar.activation(sd[:, 0:T], var[:, 0:T], ACT.Sqrt), f"sd:{p}")

            def ffn(f, p=None, gain=None):
                T = ftok(f)
                if f != 2:
                    root(f"f{f}", T)
                for part, n in enumerate(PAIRS):
                    st = f"gu{f}{part}"
                    u = U0[st] + RING

                    def gu(it, i, ix):
                        for half, names in enumerate((("u0", "gate1"), ("u2", "up1"))):
                            for e in range(2):
                                split(u + 2 * half + e, i, f"{st}:{it}:{names[e]}", ix)
                            for j in range(2):
                                if half == 0:
                                    on_dve(f"{st}:{it}:g{j}", ix)
                                    fn(nc.scalar.activation(t2[:, j, 0:T], t1[:, j, 0:T], ACT.Silu),
                                       f"{st}:{it}:silu{j}")
                                else:
                                    on_dve(f"rd:{st}:{it}:up{j}", ix)
                                    fn(nc.scalar.activation(
                                        aH[:, bass.ds(2 * i + j, 1), 0:T] if it == "L" else aH[:, j:j + 1, 0:T],
                                        m[:, j:j + 1, 0:T], ACT.Copy), f"{st}:{it}:ah{j}")

                    gu("0", 0, 0)
                    with act.Fori(1, n) as i:
                        C.enter("act", st, i - 1)
                        gu("L", i, i - 1)
                        C.leave("act", n - 1)
                    st = f"dn{f}{part}"
                    for dg in range(2):
                        for j in range(n):
                            if j < n - 1:
                                after(st, dg * n + j, f"{st}:u{dg * n + j}")
                        if part == 1 and p:
                            for k in range(4 * dg, 4 * dg + 4):
                                prep(p, k, gain, T)
                        after(st, dg * n + n - 1, f"{st}:{4 * dg + 3}")

            for u in range(RING):
                split(u)
            for k in range(KD):
                prep("f0", k, (1, "ffn1_norm"), T1)
            ffn(0, "pool", (1, "mix_norm"))
            root("pool", T1)
            for j in range(2):
                after("pool", j, f"pool:{4 * j + 3}")
                for k in range(4 * j, 4 * j + 4):
                    prep("f1", k, (1, "ffn2_norm"), T1)
            ffn(1, "dkv", (1, "kv_in_norm"))
            root("dkv", T1)
            for j in range(4):
                after("dkv", j, f"dkv:u{j}" if j < 3 else "dkv:3")
            for k in range(KD):
                fn(nc.scalar.activation(xH[:, k, :], h[:, k, :], ACT.Copy,
                                        scale=gcol(1, "ffn1_norm", KD + k)), f"xh:f2:{k}")
            ffn(2, "dq", (1, "mix_norm1"))

            after("dq", 0, "dq:0")
            after("dq", 1, "dq:1")
            root("dq", T1)
            on_dve(f"ss:dq:{KD - 1}")
            for k in range(KKV):
                fn(nc.scalar.activation(sq[:, k, :], clat[:, k, :], ACT.Square), f"sq:kv:{k}")
            for k in range(KQ):
                on_dve(f"rd:dq:{k}")
                fn(nc.scalar.activation(cqH[:, k, :], cqr[:, k, :], ACT.Copy,
                                        scale=gcol(1, "q_latent_norm", k)), f"cqh:{k}")
            after("dq", 2, "dq:2")
            root("kv", T1)
            for k in range(KQ):
                on_dve(f"ss:kv:{k}" if k < KKV else f"ss:cq:{k - 2}")
                fn(nc.scalar.activation(sq[:, k % 2, :], cqr[:, k, :], ACT.Square), f"sq:cq:{k}")
            for k in range(KKV):
                on_dve(f"cn:{k}")
                fn(nc.scalar.activation(cnH[:, k, :], t1[:, k, :], ACT.Copy), f"cnh:{k}")
            root("cq", T1)
            for hd in range(NH):
                fn(nc.scalar.activation(kcat[DN:P, hd, :], krope[DN:P, :], ACT.Copy))
            for j in range(4):
                after("uq", j, f"uq:{2 * j + 1}")
            for hd in range(NH):
                on_pe(f"uk:{hd // 2}")
                r = hd % 2 * DN
                fn(nc.scalar.activation(pairs(kcat[0:DN, hd, :]), slot(f"uk:{hd // 2}", T1)[r:r + DN],
                                        ACT.Copy), f"kcat{hd}")
            after("uk", 0, "uk:3")
            after("uv", 0, "uv:4")
            for what, hd, i in mla_order():
                s = C.slot.get(f"mla:{what}{hd}:{i}", 0)
                if what == "S":
                    st = (hd * (NT + 1) + i) % 2
                    rows = P if i < NT else NMETA
                    lo = BANK - (i + 1) * P if i < NT else BANK
                    on_dve(f"mla:m{hd}:{i}")
                    fn(nc.scalar.activation(
                        t2[0:rows, st, lo:T1], flat(s)[0:rows, lo:T1], ACT.Exp,
                        bias=small[0:rows, 4 * st + 1:4 * st + 2], scale=SM_SCALE,
                        accum_out=small[0:rows, 4 * st + 2:4 * st + 3]), f"mla:e{hd}:{i}")
                elif what == "V":
                    on_pe(f"mla:V{hd}:{i}")
                    r = slice(hd % 2 * DV, hd % 2 * DV + DV)
                    fn(nc.scalar.activation(oH[r, hd // 2, NMETA:], ps[r, 2 * s, :], ACT.Copy))
                    fn(nc.scalar.activation(oH[r, hd // 2, 0:NMETA], ps[r, 2 * s + 1, 0:NMETA],
                                            ACT.Copy), f"oh{hd}")
            for j in range(4):
                after("wo", j, f"wo:{2 * j + 1}")
                for d in (2 * j, 2 * j + 1):
                    prep("f3", d, (1, "ffn2_norm1"), T1)
            ffn(3, "final", None)
            root("final", T1)

            for k in range(KD):
                prep("b2", k, (2, "mix_norm_g_2"), SEQ)
            def head_roots(n):
                for f in (2 * n, 2 * n + 1):
                    on_dve(f"rd:st:qk:{f}")
                    fn(nc.scalar.activation(m[:, f % 2, 0:SEQ], t2[:, f % 2, 0:SEQ], ACT.Sqrt), f"sd:qk:{f}")

            for n in range(4):
                after("qk", 2 * n, f"qk:u{U0['qk'] + 2 * n}")
                after("qk", 2 * n + 1, f"qk:{2 * n + 1}")
                if n == 0:
                    root("b2", SEQ)
                for f in (2 * n, 2 * n + 1):
                    on_dve(f"rd:qk:{f}")
                    if f >= 2:
                        on_pe(f"st:qk:{f - 2}")
                    fn(nc.scalar.activation(sq[:, f % 2, 0:SEQ], (q2, k2)[f // 4][:, f % 4, :], ACT.Square),
                       f"sq:qk:{f}")
                if n:
                    head_roots(n - 1)
            head_roots(3)
            for j in range(4):
                after("v", j, f"v:u{j}" if j < 3 else "v:3")

            def query(hd):
                on_dve(f"qz{hd}")
                r = slice(hd % 2 * DV, hd % 2 * DV + DV)
                fn(nc.scalar.activation(qpad[r, :], q2[r, hd // 2, :], ACT.Copy), f"qpad{hd}")

            def softplus(hd):
                for j in reversed(range(NT)):
                    on_pe(f"z{hd}:{j}")
                    fn(nc.scalar.activation(spl(j), ps[:, 2 * j + 1, 0:SEQ - j * P], ACT.Abs), f"abs{hd}:{j}")
                    act.wait_ge(act_done, at("act", f"abs{hd}:{j}"))
                    fn(nc.scalar.activation(spl(j), spl(j), ACT.Exp, scale=-1.0), f"exp{hd}:{j}")
                for j in reversed(range(NT)):
                    act.wait_ge(act_done, at("act", f"exp{hd}:{j}"))
                    fn(nc.scalar.activation(spl(j), spl(j), ACT.Ln, bias=ones[:, 0:1]), f"ln{hd}:{j}")

            query(0)
            for what, *at_ in blend_order():
                if what == "z":
                    softplus(*at_)
                elif what == "r":
                    hd, = at_
                    for j in reversed(range(NT)):
                        on_pe(f"r{hd}:{j}")
                        fn(nc.scalar.activation(attn(j), ps[:, 2 * j + 1, 0:SEQ - j * P], ACT.Exp), f"a{hd}:{j}")
                elif what == "o":
                    if at_[0] + 1 < NH:
                        query(at_[0] + 1)
                else:
                    n, e, f = at_
                    if f == 1:
                        after(what, 2 * n + e, f"{what}:{2 * n + 1}" if e else f"{what}:u{U0[what] + 2 * n}")
                    if what == "cf" and n % 2 and e == f == 1:
                        for x in range(2):
                            on_dve(f"rd:cf:{2 * n + x}")
                            fn(nc.scalar.activation(m[:, x, 0:SEQ], t2[:, x, 0:SEQ], ACT.Sigmoid),
                               f"sig:cf:{2 * n + x}")
            for c in range(CT):
                on_dve(f"rd:o2:{2 * c + 1}")
                fn(nc.scalar.activation(o2H[:, c, :], o2[:, c, :], ACT.Copy), f"o2h{c}")

            def layer_norm(p):
                if p == 1:
                    for c in range(CT):
                        on_dve(f"cm:{c}")
                        if c >= 2:
                            on_dve(f"ss:ln:{c - 2}")
                        fn(nc.scalar.activation(sq[:, c % 2, 0:SEQ], conv[:, c, :], ACT.Square), f"sq:ln:{c}")
                elif p == 2:
                    on_dve("rd:st:lnv")
                    fn(nc.scalar.activation(sd[:, 0:SEQ], var[:, 0:SEQ], ACT.Sqrt), "sd:ln")
                elif p == 3:
                    for c in range(CT):
                        on_dve(f"ln:{c}")
                        fn(nc.scalar.activation(hbn[:, c % 2, 0:SEQ], lnt[:, c % 2, 0:SEQ], ACT.Silu,
                                                bias=gcol(2, "conf_ln_b_2", c), scale=gcol(2, "conf_ln_g_2", c)),
                           f"hbn{c}")
                        act.wait_ge(act_done, at("act", f"hbn{c}"))
                        fn(nc.scalar.activation(hbH[:, c, :], hbn[:, c % 2, 0:SEQ], ACT.Copy), f"hbh{c}")
                        fn(nc.scalar.activation(hcH[:, c, :], hcr[:, c, :], ACT.Copy), f"hch{c}")

            for b in range(3):
                for p in range(4):
                    j = (b * 4 + p) * 3
                    after("br", j, f"y{b}:{2 * p + 1}")
                    after("br", j + 1, f"gate{b}:u{U0['br'] + j + 1}")
                    after("br", j + 2, f"gate{b}:{2 * p + 1}")
                    for e in range(2):
                        d = 2 * p + e
                        on_dve(f"rd:gate{b}:{d}")
                        fn(nc.scalar.activation(t2[:, e, 0:SEQ], t1[:, e, 0:SEQ], ACT.Sigmoid,
                                                bias=gcol(2, "gate_b_2", b * KD + d)), f"sig{b}:{d}")
                        if b == 2:
                            on_dve(f"mg:{d}")
                            fn(nc.scalar.activation(mgH[:, d, :], merged[:, d, :], ACT.Copy), f"mgh:{d}")
                    if b == 0:
                        layer_norm(p)
            for p in range(4):
                after("wo2", 2 * p, f"wo2:u{U0['wo2'] + 2 * p}")
                after("wo2", 2 * p + 1, f"wo2:{2 * p + 1}")
                for d in (2 * p, 2 * p + 1):
                    prep("f4", d, (2, "ffn_norm_g_2"), SEQ)
            ffn(4)

        @block.vector
        def _(dve):
            V = nc.vector

            def do(ins, *names):
                ins.then_inc(dve_done, 1)
                C.tick("dve", *names)

            def own(name=None):
                dve.wait_ge(dve_done, at("dve", name) if name else C.here("dve"))

            def on_act(name, i=0):
                dve.wait_ge(act_done, at("act", name, i))

            def on_pe(name, i=0):
                dve.wait_ge(pe_done, at("pe", name, i))

            def src(p, k):
                return x2[:, k, :] if p in ("b2", "f4") else h[:, k, :]

            def prep(p, k, gain, T, squares=True):
                if squares:
                    on_act(f"sq:{p}:{k}")
                    if k == 0:
                        do(V.tensor_copy(ss[:, 0:T], sq[:, 0, 0:T]), f"ss:{p}:0")
                    else:
                        own(f"ss:{p}:{k - 1}")
                        do(V.tensor_tensor(ss[:, 0:T], ss[:, 0:T], sq[:, k % 2, 0:T], ALU.add), f"ss:{p}:{k}")
                if gain:
                    on_act(f"xh:{p}:{k}")
                    do(V.scalar_tensor_tensor(xL[:, k, 0:T], src(p, k), gcol(*gain, k), f32(xH[:, k, 0:T]),
                                              ALU.mult, ALU.subtract), f"xl:{p}:{k}")

            def variance(p, T, n):
                on_pe(f"st:{p}")
                own()
                do(V.tensor_scalar(like(var[:, 0:T], T), slot(f"st:{p}", T), 1.0 / n, EPS, ALU.mult, ALU.add),
                   f"rd:st:{p}")

            def rsqrt(r, v, s, root):
                on_act(root)
                own()
                do(V.reciprocal(r, s))
                own()
                do(V.tensor_tensor(s, r, r, ALU.mult))
                own()
                do(V.tensor_tensor(s, s, v, ALU.mult))
                own()
                do(V.tensor_scalar(s, s, -0.5, 1.5, ALU.mult, ALU.add))
                own()
                do(V.tensor_tensor(r, r, s, ALU.mult))

            def scales(p, T, n=D, r=rs):
                variance(p, T, n)
                rsqrt(r[:, 0:T], var[:, 0:T], sd[:, 0:T], f"sd:{p}")
                own()

            def scaled(out, name, T, *names):
                on_pe(name)
                do(V.tensor_tensor(like(out, T), slot(name, T), like(rs[:, 0:T], T), ALU.mult),
                   "rd:" + name, *names)

            def ffn(f, p=None, gain=None):
                T = ftok(f)
                if f != 2:
                    scales(f"f{f}", T)
                for part, n in enumerate(PAIRS):
                    st = f"gu{f}{part}"

                    def gu(it, i, ix):
                        for j in range(2):
                            name = f"{st}:{it}:gate{j}"
                            on_pe(name, ix)
                            do(V.tensor_tensor(like(t1[:, j, 0:T], T), slot(name, T), like(rs[:, 0:T], T),
                                               ALU.mult), "rd:" + name, f"{st}:{it}:g{j}")
                        for j in range(2):
                            name = f"{st}:{it}:up{j}"
                            on_pe(name, ix)
                            on_act(f"{st}:{it}:silu{j}", ix)
                            own()
                            do(V.tensor_tensor(like(m[:, j, 0:T], T), slot(name, T), like(t2[:, j, 0:T], T),
                                               ALU.mult), "rd:" + name)
                        for j in range(2):
                            on_act(f"{st}:{it}:ah{j}", ix)
                            fl = bass.ds(2 * i + j, 1) if it == "L" else slice(j, j + 1)
                            do(V.tensor_tensor(aL[:, fl, 0:T], m[:, j:j + 1, 0:T], f32(aH[:, fl, 0:T]),
                                               ALU.subtract), f"{st}:{it}:lo{j}")

                    gu("0", 0, 0)
                    with dve.Fori(1, n) as i:
                        C.enter("dve", st, i - 1)
                        gu("L", i, i - 1)
                        C.leave("dve", n - 1)
                    last = part == 1
                    for d in range(KD):
                        name = f"dn{f}{part}:{d}"
                        on_pe(name)
                        own()
                        do(V.scalar_tensor_tensor(like(m[:, d % 2, 0:T], T), slot(name, T),
                                                  0.5 if f < 4 else 1.0, like(rs[:, 0:T], T),
                                                  ALU.mult, ALU.mult), "rd:" + name)
                        own()
                        hd = x2[:, d, :] if f == 4 else h[:, d, :]
                        do(V.tensor_tensor(hd, hd, m[:, d % 2, 0:T], ALU.add),
                           *([f"h:{p or 'f4out'}:{d}"] if last else []))
                        if last and p and d:
                            prep(p, d - 1, gain, T)
                    if last and p:
                        prep(p, KD - 1, gain, T)

            for n, (g, rows) in enumerate(((g1, N1), (g2, N2), (g3, N3))):
                on_pe(f"g{n}")
                do(V.tensor_copy(g[:, :], slot(f"g{n}", rows)), f"rd:g{n}")
            own()
            do(V.tensor_scalar(gcol(2, "q_norm_g_2", 0), gcol(2, "q_norm_g_2", 0), 1 / np.sqrt(DV), None,
                               ALU.mult))
            for k in range(KD):
                on_pe(f"in{k}")
                s = 2 * C.slot.get(f"in{k}", 0)
                do(V.tensor_copy(h[:, k, 0:NMETA], ps[:, s + 1, 0:NMETA]))
                do(V.tensor_copy(h[:, k, NMETA:], ps[:, s, :]), f"rd:in{k}", f"h:f0:{k}")
                if k:
                    prep("f0", k - 1, (1, "ffn1_norm"), T1)
            prep("f0", KD - 1, (1, "ffn1_norm"), T1)
            ffn(0, "pool", (1, "mix_norm"))

            own()
            do(V.memset(zpad[:, 0:PAD], 0.0))
            do(V.memset(wpad[:, :, 0:PAD], 0.0))
            scales("pool", T1)
            for d in range(KD):
                g = d // 2
                scaled(zpad[:, PAD:], f"pool:{d}", T1)
                a = zpad
                for step in range(g + 1):
                    b = wpad[:, step % 2, :]
                    sh = PAD - (1 << step)
                    own()
                    do(V.tensor_tensor(b[:, PAD:], a[:, PAD:], a[:, sh:sh + T1], ALU.add))
                    a = b
                own()
                cnt = cst[:, C_CNT + g * NMETA:C_CNT + (g + 1) * NMETA]
                do(V.tensor_tensor(a[:, PAD:PAD + NMETA], a[:, PAD:PAD + NMETA], cnt, ALU.mult))
                own()
                do(V.scalar_tensor_tensor(zpad[:, PAD:], a[:, PAD:], 1.0 / POOL_W[g], zpad[:, PAD:],
                                          ALU.mult, ALU.subtract))
                own()
                do(V.scalar_tensor_tensor(h[:, d, :], zpad[:, PAD:], gcol(1, "pool_scale", d), h[:, d, :],
                                          ALU.mult, ALU.add), f"h:f1:{d}")
                if d:
                    prep("f1", d - 1, (1, "ffn2_norm"), T1)
                own()
            prep("f1", KD - 1, (1, "ffn2_norm"), T1)
            ffn(1, "dkv", (1, "kv_in_norm"))

            scales("dkv", T1)
            for d in range(KKV):
                scaled(clat[:, d, :], f"dkv:{d}", T1)
            dve.wait_ge(s_t, 16)
            for d, t in ((2, TAB_COS), (3, TAB_SIN)):
                on_pe(f"dkv:{d}")
                do(V.tensor_tensor(pairs(m[:, d - 2, :]), slot(f"dkv:{d}", T1), pairs(tab[:, t, :]), ALU.mult),
                   f"rd:dkv:{d}")
            for k in range(KD):
                prep("f2", k, (1, "ffn1_norm1"), T1, squares=False)
            own()
            do(V.tensor_tensor(m[:, 0, :], m[:, 0, :], m[:, 1, :], ALU.add))
            own()
            do(V.tensor_tensor(krope[:, :], m[:, 0, :], rs[:, :], ALU.mult), "krope")
            ffn(2, "dq", (1, "mix_norm1"))

            scales("dq", T1)
            for k in range(KQ):
                scaled(cqr[:, k, :], f"dq:{k}", T1)

            def add_square(p, k, T):
                on_act(f"sq:{p}:{k}")
                own()
                if k == 0:
                    do(V.tensor_copy(ss[:, 0:T], sq[:, 0, 0:T]), f"ss:{p}:0")
                else:
                    do(V.tensor_tensor(ss[:, 0:T], ss[:, 0:T], sq[:, k % 2, 0:T], ALU.add), f"ss:{p}:{k}")

            for k in range(KKV):
                add_square("kv", k, T1)
            for k in range(KQ):
                on_act(f"cqh:{k}")
                do(V.scalar_tensor_tensor(cqL[:, k, :], cqr[:, k, :], gcol(1, "q_latent_norm", k),
                                          f32(cqH[:, k, :]), ALU.mult, ALU.subtract), f"cql:{k}")
            variance("kv", T1, RKV)
            for k in range(KQ):
                add_square("cq", k, T1)
            rsqrt(rl[:, :], var[:, :], sd[:, :], "sd:kv")
            own()
            for k in range(KKV):
                do(V.scalar_tensor_tensor(t1[:, k, :], clat[:, k, :], gcol(1, "kv_latent_norm", k), rl[:, :],
                                          ALU.mult, ALU.mult), f"cn:{k}")
            for k in range(KKV):
                on_act(f"cnh:{k}")
                do(V.tensor_tensor(cnL[:, k, :], t1[:, k, :], f32(cnH[:, k, :]), ALU.subtract), f"cnl:{k}")
            scales("cq", T1, RQ, rl)
            do(V.tensor_tensor(ss[:, :], tab[:, TAB_Q, :], rl[:, :], ALU.mult))
            do(V.memset(vmeta[:, :], 0.0))
            do(V.memset(pmT[:, :], 0.0))
            own()
            for hd in range(NH):
                on_pe(f"uq:{hd}")
                do(V.tensor_tensor(pairs(qcat[:, hd, :]), slot(f"uq:{hd}", T1), pairs(ss[:, :]), ALU.mult),
                   f"rd:uq:{hd}", f"qcat{hd}")
            for t in range(NT + 1):
                on_pe(f"uv:{t}")
                if t < NT:
                    do(V.tensor_copy(vreal[:, t, :], slot(f"uv:{t}", SEQ)), f"rd:uv:{t}")
                else:
                    do(V.tensor_copy(vmeta[0:NMETA, :], slot(f"uv:{t}", SEQ)[0:NMETA]), f"rd:uv:{t}")
            order = mla_order()
            steps = [(hd, i) for what, hd, i in order if what == "S"]

            def normalise(hd, i):
                st = (hd * (NT + 1) + i) % 2
                rows = P if i < NT else NMETA
                lo = BANK - (i + 1) * P if i < NT else BANK
                on_act(f"mla:e{hd}:{i}")
                do(V.reciprocal(small[0:rows, 4 * st + 3:4 * st + 4], small[0:rows, 4 * st + 2:4 * st + 3]))
                n = hd * (NT + 1) + i
                if n >= 4:
                    on_pe(f"mla:T{steps[n - 4][0]}:{steps[n - 4][1]}")
                own()
                do(V.tensor_scalar(prob[0:rows, n % 4, lo:T1], t2[0:rows, st, lo:T1],
                                   small[0:rows, 4 * st + 3:4 * st + 4], None, ALU.mult),
                   f"mla:p{hd}:{i}", f"rd:mla:S{hd}:{i}")

            behind = None
            for what, hd, i in order:
                s = C.slot.get(f"mla:{what}{hd}:{i}", 0)
                if what == "S":
                    st = (hd * (NT + 1) + i) % 2
                    rows = P if i < NT else NMETA
                    lo = BANK - (i + 1) * P if i < NT else BANK
                    on_pe(f"mla:S{hd}:{i}")
                    if i < NT:
                        do(V.memset(flat(s)[0:P // 2, BANK - P // 2:BANK], NEG))
                        own()
                    do(V.tensor_reduce(small[0:rows, 4 * st:4 * st + 1], flat(s)[0:rows, lo:T1], AX_X, ALU.max))
                    own()
                    do(V.tensor_scalar(small[0:rows, 4 * st + 1:4 * st + 2], small[0:rows, 4 * st:4 * st + 1],
                                       -SM_SCALE, None, ALU.mult), f"mla:m{hd}:{i}")
                    if behind:
                        normalise(*behind)
                    behind = (hd, i)
                elif what == "T":
                    if behind and (hd, i) == steps[-3]:
                        normalise(*behind)
                        behind = None
                    on_pe(f"mla:T{hd}:{i}")
                    if hd:
                        on_pe(f"mla:V{hd - 1}:0")
                    b0, b1 = ps[:, 2 * s, :], ps[:, 2 * s + 1, :]
                    if i < NT:
                        do(V.tensor_copy(pT[:, 0:i + 1, i * P:(i + 1) * P],
                                         b0[:, 0:(i + 1) * P].rearrange("p (j q) -> p j q", j=i + 1)))
                        do(V.tensor_copy(pmT[0:NMETA, NMETA + i * P:NMETA + (i + 1) * P], b1[0:NMETA, 0:P]),
                           f"rd:mla:T{hd}:{i}")
                    else:
                        do(V.tensor_copy(pmT[0:NMETA, 0:NMETA], b1[0:NMETA, 0:NMETA]), f"rd:mla:T{hd}:{i}")
                else:
                    on_act(f"oh{hd}")
                    r = slice(hd % 2 * DV, hd % 2 * DV + DV)
                    do(V.tensor_tensor(oL[r, hd // 2, NMETA:], ps[r, 2 * s, :], f32(oH[r, hd // 2, NMETA:]),
                                       ALU.subtract))
                    do(V.tensor_tensor(oL[r, hd // 2, 0:NMETA], ps[r, 2 * s + 1, 0:NMETA],
                                       f32(oH[r, hd // 2, 0:NMETA]), ALU.subtract),
                       f"ol{hd}", f"rd:mla:V{hd}:0")
            for d in range(KD):
                on_pe(f"wo:{d}")
                own()
                do(V.tensor_tensor(pairs(h[:, d, :]), slot(f"wo:{d}", T1), pairs(h[:, d, :]), ALU.add),
                   f"rd:wo:{d}", f"h:f3:{d}")
                if d:
                    prep("f3", d - 1, (1, "ffn2_norm1"), T1)
            prep("f3", KD - 1, (1, "ffn2_norm1"), T1)
            ffn(3, "final", None)

            scales("final", T1)
            for k in range(KD):
                do(V.scalar_tensor_tensor(x2[:, k, :], x2[:, k, :], gcol(1, "final_norm", k), rs[:, NMETA:],
                                          ALU.mult, ALU.mult), f"h:b2:{k}")
                if k:
                    prep("b2", k - 1, (2, "mix_norm_g_2"), SEQ)
            prep("b2", KD - 1, (2, "mix_norm_g_2"), SEQ)

            scales("b2", SEQ)

            def head_norm(n):
                for f in (2 * n, 2 * n + 1):
                    on_pe(f"st:qk:{f}")
                    own()
                    do(V.tensor_scalar(t2[:, f % 2, 0:SEQ], slot(f"st:qk:{f}", SEQ), 1.0 / DV, EPS,
                                       ALU.mult, ALU.add), f"rd:st:qk:{f}")
                for f in (2 * n, 2 * n + 1):
                    rsqrt(t1[:, f % 2, 0:SEQ], t2[:, f % 2, 0:SEQ], m[:, f % 2, 0:SEQ], f"sd:qk:{f}")
                    own()
                    t = (q2, k2)[f // 4][:, f % 4, :]
                    do(V.scalar_tensor_tensor(t, t, gcol(2, ("q_norm_g_2", "k_norm_g_2")[f // 4], 0),
                                              t1[:, f % 2, 0:SEQ], ALU.mult, ALU.mult), f"qkn{f}")

            for n in range(4):
                for f in (2 * n, 2 * n + 1):
                    scaled((q2, k2)[f // 4][:, f % 4, :], f"qk:{f}", SEQ)
                if n:
                    head_norm(n - 1)
            head_norm(3)
            on_pe("rcol")
            do(V.tensor_copy(small[:, 0:NT], slot("rcol", SEQ)[:, 0:NT]), "rd:rcol")
            do(V.memset(hb[:, :, 0:CONV - 1], 0.0))
            do(V.memset(xc[:, :, 0:SCW - 1], 0.0))
            do(V.memset(qpad[DV:P, :], 0.0), "qz0")
            own()
            for t in range(NT):
                on_pe(f"v:{t}")
                do(V.tensor_scalar(v2[:, t, :], slot(f"v:{t}", SEQ), small[:, t:t + 1], None, ALU.mult),
                   f"rd:v:{t}")

            def cf(n):
                own()
                for e in range(2):
                    scaled((t1, t2)[n % 2][:, e, 0:SEQ], f"cf:{2 * n + e}", SEQ)
                if n % 2:
                    for e in range(2):
                        on_act(f"sig:cf:{2 * n + e}")
                        do(V.tensor_tensor(hb[:, n - 1 + e, CONV - 1:], t1[:, e, 0:SEQ], m[:, e, 0:SEQ], ALU.mult))
                    own()

            tapped = [0]

            def taps(n):
                for i in range(tapped[0], min(tapped[0] + n, CONV * CT)):
                    tap, c = i // CT, i % CT
                    wt = g3[:, i:i + 1]
                    name = f"conv{tap}:{c}" if i < CONV * CT - 1 else "conv"
                    if tap == 0:
                        do(V.tensor_scalar(conv[:, c, :], hb[:, c, 0:SEQ], wt, gcol(2, "conf_dw_b_2", c),
                                           ALU.mult, ALU.add), name)
                    else:
                        own(f"conv{tap - 1}:{c}")
                        do(V.scalar_tensor_tensor(conv[:, c, :], hb[:, c, tap:tap + SEQ], wt, conv[:, c, :],
                                                  ALU.mult, ALU.add), name)
                tapped[0] += n

            def sc(n):
                p, part = n // 3, n % 3
                own()
                for e in range(2):
                    scaled((t1, t2, t1)[part][:, e, 0:SEQ], f"sc:{2 * n + e}", SEQ)
                own()
                if part == 1:
                    for e in range(2):
                        do(V.tensor_tensor(xc[:, e, SCW - 1:], t1[:, e, 0:SEQ], t2[:, e, 0:SEQ], ALU.mult))
                    own()
                    for tap in range(SCW):
                        for e in range(2):
                            r = G2["sc_conv_w_2"][0] + tap * CT + 2 * p + e
                            wt = g2[:, r:r + 1]
                            if tap == 0:
                                do(V.tensor_scalar(m[:, e, 0:SEQ], xc[:, e, 0:SEQ], wt, None, ALU.mult))
                            else:
                                do(V.scalar_tensor_tensor(m[:, e, 0:SEQ], xc[:, e, tap:tap + SEQ], wt,
                                                          m[:, e, 0:SEQ], ALU.mult, ALU.add))
                        own()
                elif part == 2:
                    for e in range(2):
                        do(V.tensor_tensor(hcr[:, 2 * p + e, :], t1[:, e, 0:SEQ], m[:, e, 0:SEQ], ALU.mult))

            for what, *at_ in blend_order():
                if what == "r":
                    hd, = at_
                    for j in reversed(range(NT)):
                        on_act(f"ln{hd}:{j}")
                        do(V.scalar_tensor_tensor(spl(j), ps[:, 2 * j + 1, 0:SEQ - j * P], 0.0, spl(j),
                                                  ALU.max, ALU.add), f"sp{hd}:{j}")
                elif what == "o":
                    hd, = at_
                    r = slice(hd % 2 * DV, hd % 2 * DV + DV)
                    on_pe(f"o2:{hd}")
                    do(V.tensor_copy(o2[r, hd // 2, :], ps[r, 2 * NT - 1, :]), f"rd:o2:{hd}")
                    if hd + 1 < NH:
                        do(V.memset(qpad[r, :], 0.0), f"qz{hd + 1}")
                elif what in ("cf", "sc"):
                    n, e, f = at_
                    if e == f == 1:
                        (cf if what == "cf" else sc)(n)
                    if what == "sc":
                        taps(4)
            for c in range(CT):
                on_act(f"o2h{c}")
                do(V.tensor_tensor(o2L[:, c, :], o2[:, c, :], f32(o2H[:, c, :]), ALU.subtract), f"o2l{c}")
            taps(CONV * CT)

            def layer_norm(p):
                if p == 1:
                    on_pe("st:mean")
                    for c in range(CT):
                        do(V.scalar_tensor_tensor(conv[:, c, :], slot("st:mean", SEQ), -1.0 / CW, conv[:, c, :],
                                                  ALU.mult, ALU.add),
                           *([f"cm:{c}"] + (["rd:st:mean"] if c == CT - 1 else [])))
                    for c in range(CT):
                        add_square("ln", c, SEQ)
                elif p == 2:
                    variance("lnv", SEQ, CW)
                    rsqrt(rl[:, 0:SEQ], var[:, 0:SEQ], sd[:, 0:SEQ], "sd:ln")
                elif p == 3:
                    own()
                    for c in range(CT + 1):
                        if c < CT:
                            if c >= 2:
                                on_act(f"hbn{c - 2}")
                            do(V.tensor_tensor(lnt[:, c % 2, 0:SEQ], conv[:, c, :], rl[:, 0:SEQ], ALU.mult), f"ln:{c}")
                        if c:
                            on_act(f"hch{c - 1}")
                            do(V.tensor_tensor(hbL[:, c - 1, :], hbn[:, (c - 1) % 2, 0:SEQ], f32(hbH[:, c - 1, :]),
                                               ALU.subtract), f"hbl{c - 1}")
                            do(V.tensor_tensor(hcL[:, c - 1, :], hcr[:, c - 1, :], f32(hcH[:, c - 1, :]),
                                               ALU.subtract), f"hcl{c - 1}")

            for b in range(3):
                for p in range(4):
                    for e in range(2):
                        on_pe(f"y{b}:{2 * p + e}")
                        own()
                        do(V.tensor_copy(m[:, e, 0:SEQ], slot(f"y{b}:{2 * p + e}", SEQ)), f"rd:y{b}:{2 * p + e}")
                    for e in range(2):
                        scaled(t1[:, e, 0:SEQ], f"gate{b}:{2 * p + e}", SEQ)
                    for e in range(2):
                        d = 2 * p + e
                        on_act(f"sig{b}:{d}")
                        own()
                        if b == 0:
                            do(V.tensor_tensor(merged[:, d, :], m[:, e, 0:SEQ], t2[:, e, 0:SEQ], ALU.mult))
                        else:
                            do(V.tensor_tensor(sq[:, e, 0:SEQ], m[:, e, 0:SEQ], t2[:, e, 0:SEQ], ALU.mult))
                            own()
                            do(V.tensor_tensor(merged[:, d, :], merged[:, d, :], sq[:, e, 0:SEQ], ALU.add),
                               *([f"mg:{d}"] if b == 2 else []))
                        if b == 2:
                            on_act(f"mgh:{d}")
                            do(V.tensor_tensor(mgL[:, d, :], merged[:, d, :], f32(mgH[:, d, :]), ALU.subtract),
                               f"mgl{d}")
                    if b == 0:
                        layer_norm(p)
            for d in range(KD):
                on_pe(f"wo2:{d}")
                own()
                do(V.tensor_tensor(x2[:, d, :], slot(f"wo2:{d}", SEQ), x2[:, d, :], ALU.add),
                   f"rd:wo2:{d}", f"h:f4:{d}")
                if d:
                    prep("f4", d - 1, (2, "ffn_norm_g_2"), SEQ)
            prep("f4", KD - 1, (2, "ffn_norm_g_2"), SEQ)
            ffn(4)
            for t in range(NT):
                on_pe(f"out{t}")
                if t >= 2:
                    dve.wait_ge(s_out[t % 2], 16 * (t // 2))
                s = 2 * C.slot.get(f"out{t}", 0)
                do(V.tensor_copy(yout[:, t % 2, :].rearrange("p (c n) -> p c n", c=2), ps[:, s:s + 2, :]),
                   f"rd:out{t}", f"yout{t}")


def _constants():
    c = np.zeros((P, C_MAIN), np.float32)
    r = np.arange(P)
    c[:, C_ID:C_ID + P] = np.eye(P)
    c[:, C_NTRI:C_NTRI + P] = -(r[:, None] >= r[None, :]).astype(np.float32)
    c[:, C_NONE:C_NONE + P] = -1.0
    c[:, C_ONE:C_ONE + P] = 1.0
    c[:, C_BLK:C_BLK + P] = r[:, None] // DV == r[None, :] // DV
    c[:, C_MASK:C_MASK + P] = np.where(r[:, None] >= r[None, :], NEG, 0.0)
    for g, win in enumerate(POOL_W):
        c[:, C_CNT + g * NMETA:C_CNT + (g + 1) * NMETA] = win / np.minimum(np.arange(NMETA) + 1, win)
    t = np.ones((P, 3, T1), np.float32)
    inv = np.float32(1.0) / np.power(np.float32(10000.0), np.arange(0, DR, 2, dtype=np.float32) / np.float32(DR))
    ang = np.arange(T1, dtype=np.float32)[None, :] * inv.astype(np.float32)[:, None]
    cos, sin = np.cos(ang), np.sin(ang)
    for p in range(P):
        sign = -1.0 if p % DR < DR // 2 else 1.0
        t[p, TAB_COS] = cos[p % (DR // 2)]
        t[p, TAB_SIN] = sign * sin[p % (DR // 2)]
    t[DN:DQK, TAB_Q] = t[DN:DQK, TAB_COS]
    t[DQK:, TAB_Q] = t[DQK:, TAB_SIN]
    return c, t


def kernel(**inputs):
    import concourse.bacc as _bacc
    from concourse.bass_utils import run_bass_kernel_spmd as _run

    arrays = {f"in_{n}": np.ascontiguousarray(a) for n, a in inputs.items()}
    arrays["consts"], arrays["tables"] = _constants()

    def build(C):
        nc = _bacc.Bacc("TRN2", target_bir_lowering=False, num_devices=1)
        aps = {n: nc.dram_tensor(n, a.shape, F32, kind="ExternalInput").ap() for n, a in arrays.items()}
        out = nc.dram_tensor("out", (1, SEQ, D), F32, kind="ExternalOutput").ap()
        program(nc, {n: aps[f"in_{n}"] for n in inputs}, out, aps["consts"], aps["tables"], C)
        return nc

    C = Counts()
    build(C)
    C.known = True
    nc = build(C)
    r = _run(nc, [arrays], core_ids=[0])
    return r.results[0]["out"]
```

```python
from contextlib import ExitStack

import numpy as np

import concourse.bass as bass
from concourse import mybir

F32 = mybir.dt.float32
F32R = mybir.dt.float32r
ALU = mybir.AluOpType
ACT = mybir.ActivationFunctionType
AX_X = mybir.AxisListType.X

P = 128
D = 1024
KD = D // P
SEQ = 512
NT = SEQ // P
NMETA = 16
T1 = SEQ + NMETA
HALF = T1 // 2
FF = 2816
PAIRS = (6, 5)
FMAX = 2 * max(PAIRS)
NH, DN, DR, DV = 8, 64, 32, 64
DQK = DN + DR
RKV, RQ = 256, 384
KKV, KQ = RKV // P, RQ // P
EPS = 1e-6
SM_SCALE = float(1.0 / np.sqrt(DQK))
SEC = {"q": 0, "k": 512, "v": 1024, "cv": 1536, "cg": 2048, "sx": 2560, "sb": 3072, "sc": 3584,
       "gate": 4096}
CW = 512
CT = CW // P
CONV, SCW = 31, 3
POOL_PACE = 2
RING = 4
UW = 1024
SLOTS = 4
BANK = 512
NEG = -1.0e30
POOL_W = (2, 4, 8, 16)

C_ID, C_NTRI, C_NONE, C_ONE, C_HEAD, C_MASK = (i * P for i in range(6))
C_MAIN = 6 * P
BAND = 2 * P
ZSTEP = P - POOL_W[-1]
TAB_Q, TAB_COS, TAB_SIN = range(3)

GAIN = {}


for _n, _k in (("ffn1_norm", 16), ("mix_norm", 16), ("ffn2_norm", 16), ("pool_scale", 8),
               ("kv_in_norm", 8), ("kv_latent_norm", 2), ("q_latent_norm", 3), ("final_norm", 8),
               ("mix_norm_g_2", 8), ("q_norm_g_2", 1), ("k_norm_g_2", 1), ("conf_dw_b_2", 4),
               ("conf_ln_g_2", 4), ("conf_ln_b_2", 4), ("sc_conv_w_2", 12), ("gate_b_2", 24),
               ("ffn_norm_g_2", 8), ("conf_dw_w_2", CONV * CT)):
    GAIN[_n] = sum(n for _, n in GAIN.values()), _k
NGAIN = sum(n for _, n in GAIN.values())


class Counts:

    def __init__(self):
        self.value, self.stride, self.slot, self.known = {}, {}, {}, False

    def start(self):
        self.n = {"pe": 0, "dve": 0, "act": 0}
        self.loop = {"pe": None, "dve": None, "act": None}

    def tick(self, eng, *names):
        self.n[eng] += 1
        for name in names:
            assert self.known or (eng, name) not in self.value, name
            self.value[eng, name] = self.n[eng]
            if self.loop[eng]:
                self.loop[eng][2].append(name)

    def also(self, eng, name):
        self.value[eng, name] = self.n[eng]

    def at(self, eng, name, i=0):
        if not self.known:
            return 1
        v = self.value[eng, name]
        return v + self.stride[eng, name] * i if (eng, name) in self.stride else v

    def here(self, eng):
        lp = self.loop[eng]
        return self.n[eng] + (lp[0] * lp[1] if lp else 0)

    def enter(self, eng, key, i):
        stride = self.stride.get((eng, "loop:" + key), 1)
        self.loop[eng] = (i, stride, [], self.n[eng], key)

    def leave(self, eng, count):
        _, _, names, first, key = self.loop[eng]
        body = self.n[eng] - first
        self.stride[eng, "loop:" + key] = body
        for name in names:
            self.stride[eng, name] = body
            if eng != "pe":
                assert self.value[eng, name] - body == self.value[eng, name.replace(":L:", ":0:")]
        self.n[eng] = first + body * count
        self.loop[eng] = None


def units():
    out = []

    def ffn(f):
        for part, pairs in enumerate(PAIRS):
            for j in range(4 * pairs):
                out.append((f"gu{f}{part}", j))
            for j in range(2 * pairs):
                out.append((f"dn{f}{part}", j))

    def stage(name, n):
        out.extend((name, j) for j in range(n))

    ffn(0)
    stage("pool", 2)
    ffn(1)
    stage("dkv", 4)
    ffn(2)
    for name, n in (("dq", 3), ("uk", 1), ("uv", 1), ("uq", 4), ("wo", 4)):
        stage(name, n)
    ffn(3)
    for name, n in (("qk", 8), ("v", 4), ("cf", 8), ("sc", 12), ("br", 36), ("wo2", 8)):
        stage(name, n)
    ffn(4)
    return out


UNITS = units()
NUNITS = len(UNITS)

U0 = {}
for _u, (_s, _j) in enumerate(UNITS):
    U0.setdefault(_s, _u)


POOL_FROM = U0["sc"]


def tap_count(tap):
    return 2 * tap + 1


RAW_AT = [16 * (u // RING + 1) for u in range(NUNITS)]


def first_order():
    order = [(k, "input") for k in range(4)]
    for k in range(0, 4, 2):
        order += [(k, "square"), (k + 1, "square"), (k + 4, "input"), (k + 5, "input")]
    return order + [(k, "square") for k in range(4, KD)]


def mla_order():
    steps = [(h, i) for h in range(NH) for i in range(NT)]
    order = []
    for s in range(len(steps) + 3):
        if s < len(steps):
            order.append(("S",) + steps[s])
        if s >= 3:
            hd, i = steps[s - 3]
            if i == 2 and hd:
                order.append(("V", hd - 1, 0))
            order.append(("T",) + steps[s - 3])
    return order + [("V", NH - 1, 0)]


def blend_order():
    quarters = [(st, n, e, f) for st, pairs in (("cf", 4), ("sc", 6)) for n in range(pairs)
                for e in range(2) for f in range(2)]
    after = {"z": 3, "r": 1, "o": 1}
    order = [quarters.pop(0)]
    for hd in range(NH):
        for what, n in after.items():
            order.append((what, hd))
            order += quarters[:n]
            del quarters[:n]
    return order + quarters


def program(nc, w, out, C):
    C.start()
    at = C.at
    ctx = ExitStack()
    with ctx:
        def sem(name):
            return ctx.enter_context(nc.semaphore(name))

        top = [nc.sbuf_base if not callable(nc.sbuf_base) else nc.sbuf_base()]
        limit = nc.sbuf_usable_end if not callable(nc.sbuf_usable_end) else nc.sbuf_usable_end()

        def place(name, shape, dt=F32, at=None):
            size = int(np.prod(shape[1:])) * 4
            size = (size + 31) // 32 * 32
            if at is None:
                at = top[0]
                top[0] += size
                assert top[0] <= limit, (name, top[0], limit)
            return nc.alloc_sbuf_tensor_at(name, list(shape), dt, offset=at)

        def zone(size):
            at = top[0]
            top[0] += (size + 31) // 32 * 32
            assert top[0] <= limit, (size, top[0], limit)
            return at

        top[0] = (top[0] + 31) // 32 * 32
        raw = place("raw", [P, RING, UW])
        wH = place("wH", [P, RING, UW], F32R)
        wL = place("wL", [P, RING, UW], F32R)
        h = place("h", [P, KD, T1])
        x2 = h[:, :, NMETA:T1]
        cst = place("cst", [P, C_MAIN])
        gains = place("gains", [P, NGAIN])
        gblk = place("gblk", [P, KD])
        rs = place("rs", [P, T1])
        rl = place("rl", [P, T1])
        hbn_at = top[0]
        var = place("var", [P, T1])
        ss = place("ss", [P, T1])
        sd = place("sd", [P, T1])
        z1 = top[0]
        t1 = place("t1", [P, 2, T1])
        t2 = place("t2", [P, 2, T1])
        m = place("m", [P, 2, T1])
        sq = place("sq", [P, 2, T1])
        small = place("small", [P, 16 + 3 * NH])
        zx = zone(KD * T1 * 8)
        xH = place("xH", [P, KD, T1], F32R, zx)
        xL = place("xL", [P, KD, T1], F32R, zx + KD * T1 * 4)
        za = zone(FMAX * T1 * 8)
        aH = place("aH", [P, FMAX, T1], F32R, za)
        aL = place("aL", [P, FMAX, T1], F32R, za + FMAX * T1 * 4)
        zs = zone(KD * SEQ * 4)
        clat = place("clat", [P, KKV, T1], F32, zs)
        krope = place("krope", [P, T1], F32, zs + KKV * T1 * 4)
        tab = place("tab", [P, 3, T1], F32, zs + 3 * T1 * 4)
        cqH = place("cqH", [P, KQ, T1], F32R, za)
        cqL = place("cqL", [P, KQ, T1], F32R, za + KQ * T1 * 4)
        oH = place("oH", [P, NH // 2, T1], F32R, za)
        oL = place("oL", [P, NH // 2, T1], F32R, za + NH // 2 * T1 * 4)
        zq = za + NH * T1 * 4
        qcat = place("qcat", [P, NH, T1], F32, zq)
        zv = zq + NH * T1 * 4
        vreal = place("vreal", [P, NT, NH * DV], F32, zv)
        vmeta = place("vmeta", [P, NH * DV], F32, zv + NT * NH * DV * 4)
        pmT = place("pmT", [P, 2, SEQ], F32, zv + (NT + 1) * NH * DV * 4)
        cnH = place("cnH", [P, KKV, T1], F32R, zq)
        cnL = place("cnL", [P, KKV, T1], F32R, zq + KKV * T1 * 4)
        kcat = place("kcat", [P, NH, T1], F32, zx)
        pT = place("pT", [P, 2, NT, SEQ], F32, zx + NH * T1 * 4)
        metaT = place("metaT", [P, NH * NMETA], F32, z1)
        metaP = place("metaP", [P, 2, NH, NMETA], F32, z1 + NH * NMETA * 4)
        prob = place("prob", [P, 4, T1], F32, z1 + 4 * T1 * 4)
        hbw = CONV - 1 + SEQ
        scw = SCW - 1 + SEQ
        zc = za + 2 * CT * SEQ * 4
        zk = zc + 2 * CT * SEQ * 4
        hb = place("hb", [P, CT, hbw], F32, za)
        xc = place("xc", [P, 2, scw], F32, z1 + 6 * T1 * 4)
        tri = [sum(SEQ - i * P for i in range(j)) for j in range(NT + 1)]
        spls = place("spls", [P, tri[NT]], F32, za + CT * hbw * 4)
        tapped = place("tapped", [P, SEQ], F32, za + (CT * hbw + tri[NT]) * 4)[:, :]
        assert CT * hbw + tri[NT] + SEQ <= 2 * CT * SEQ
        v2 = place("v2", [P, NT, CW], F32, zs)
        qpad = place("qpad", [P, SEQ], F32, zs + NT * CW * 4)
        attns = place("attns", [P, tri[NT]], F32, zs + (NT * CW + SEQ) * 4)
        heads = place("heads", [P, 2 * NH * DV], F32, zs + (NT * CW + SEQ) * 4)
        maskR = place("maskR", [P, 2, P], F32R, zs + (NT * CW + SEQ + tri[NT]) * 4)
        assert NT * CW + SEQ + tri[NT] + 2 * P <= KD * SEQ
        conv = place("conv", [P, CT, SEQ], F32, zc)
        hcr = place("hcr", [P, CT, SEQ], F32, zc + CT * SEQ * 4)
        q2 = place("q2", [P, CT, SEQ], F32, zk)
        k2 = place("k2", [P, CT, SEQ], F32, zk + CT * SEQ * 4)
        o2 = q2
        o2L = place("o2L", [P, CT, SEQ], F32R, zk)
        o2H = place("o2H", [P, CT, SEQ], F32R, zk + CT * SEQ * 4)
        hbH = place("hbH", [P, CT, SEQ], F32R, za)
        hbL = place("hbL", [P, CT, SEQ], F32R, za + CT * SEQ * 4)
        hcH = place("hcH", [P, CT, SEQ], F32R, zc)
        hcL = place("hcL", [P, CT, SEQ], F32R, zc + CT * SEQ * 4)
        hbn = place("hbn", [P, 2, T1], F32, hbn_at)
        lnt = sq
        rs2 = sd
        merged = place("merged", [P, KD, SEQ], F32, zs)
        mgH = place("mgH", [P, KD, SEQ], F32R, za)
        mgL = place("mgL", [P, KD, SEQ], F32R, zk)
        zt = place("zt", [P, NT + 1, D], F32, za)
        bands = place("bands", [P, len(POOL_W), BAND], F32, zs)
        zout = [(t, min(t + ZSTEP, T1)) for t in range(0, T1, ZSTEP)]
        ztok = [slice(a, a + P) for a in (max(0, min(t - POOL_W[-1], T1 - P)) for t, _ in zout)]
        assert len(ztok) == NT + 1
        pvar, psd, prs = (small[:, 16 + i * NH:16 + i * NH + NT + 1] for i in range(3))

        def spl(j):
            return spls[:, tri[j]:tri[j + 1]]

        def later(j):
            pieces = [(P, spl(j + 1)[:, 0:P])] if j + 1 < NT else []
            a = P * sum(NT - 2 - i for i in range(j + 1, NT - 1))
            return pieces + ([(2 * P, rl[:, a:a + (NT - 2 - j) * P])] if j + 2 < NT else [])

        def attn(j):
            return attns[:, tri[j]:tri[j + 1]]

        ps = ctx.enter_context(nc.psum_tensor("ps", [P, 2 * SLOTS, BANK], F32))
        ident = cst[:, C_ID:C_ID + P]
        ntri = cst[:, C_NTRI:C_NTRI + P]
        none_ = cst[:, C_NONE:C_NONE + P]
        ones = cst[:, C_ONE:C_ONE + P]
        hsum = cst[:, C_HEAD:C_HEAD + P]
        mask = cst[:, C_MASK:C_MASK + P]

        def pairs(ap):
            return ap.rearrange("p (c n) -> p c n", c=2)

        def slot(name, T):
            s = C.slot.get(name, 0)
            return ps[:, 2 * s:2 * s + 2, 0:HALF] if T == T1 else ps[:, 2 * s, 0:T]

        def like(ap, T):
            return pairs(ap) if T == T1 else ap

        def flat(s):
            return ps[:, 2 * s:2 * s + 2, :].rearrange("p c n -> p (c n)")

        def f32(ap):
            return ap.bitcast(F32)

        def gcol(name, k):
            if name == "block2":
                return gblk[:, k:k + 1]
            if name.endswith("norm1"):
                name, k = name[:-1], k + KD
            return gains[:, GAIN[name][0] + k:GAIN[name][0] + k + 1]

        raw_in = [sem(f"raw_in{s}") for s in range(RING)]
        h_done = sem("hi_done")
        l_done = sem("lo_done")
        pe_done = sem("pe_done")
        dve_done = sem("dve_done")
        act_done = sem("act_done")
        taps_done = sem("taps_done")
        s_x = [sem(f"x_in{k}") for k in range(0, KD, 2)]
        s_c = sem("consts_in")
        s_g = sem("gains_in")
        s_t = sem("tables_in")
        s_h = sem("heads_in")
        s_b = sem("bands_in")
        s_out = sem("out_done")

        block = ctx.enter_context(nc.Block())

        def ffn_weights(f):
            if f < 4:
                a, l = ("ffn1", "ffn2")[f % 2], f // 2
                return w[a + "_w_gate"][l], w[a + "_w_up"][l], w[a + "_w_down"][l]
            wi = w["w_ffn_in_2"][0]
            return wi[:, 0:FF], wi[:, FF:2 * FF], w["w_ffn_out_2"][0]

        def ftok(f):
            return T1 if f < 4 else SEQ

        @block.sync
        def _(sp):
            def load_x(k):
                sp.dma_start(h[:, k:k + 2, :], w["tokens"][:, k:k + 2, :]).then_inc(s_x[k // 2], 16)

            def load(u, src, i=0):
                if u >= RING or not isinstance(i, int):
                    sp.wait_ge(l_done, u - RING + 1 + RING * i)
                n = src.shape[1] * src.shape[2]
                sp.dma_start(raw[:, u % RING, 0:n].rearrange("p (a b) -> p a b", a=src.shape[1]),
                             src).then_inc(raw_in[u % RING], 16)

            def kpart(wt, k0, nk, c0, c1):
                return wt[k0 * P:(k0 + nk) * P, c0:c1].rearrange("(a p) c -> p a c", p=P)

            def load_ffn(f):
                gate, up, down = ffn_weights(f)
                row = 0
                for part, n in enumerate(PAIRS):
                    u = U0[f"gu{f}{part}"]

                    def gu(i, c, first=False):
                        for j in range(4):
                            if first and j in (1, 2):
                                load_x(4 * j - 4)
                                load_x(4 * j - 2)
                            elif first and j == 3:
                                sp.dma_start(cst[:, :], w["consts"]).then_inc(s_c, 16)
                            wt = (gate, gate, up, up)[j]
                            src = wt[(j % 2) * 4 * P:(j % 2 + 1) * 4 * P, bass.ds(c, 2 * P)]
                            load(u + j, src.rearrange("(a p) c -> p a c", p=P), i)

                    gu(0, row * P, f == part == 0)
                    with sp.Fori(1, n) as i:
                        gu(i, row * P + i * (2 * P))
                    u = U0[f"dn{f}{part}"]
                    for dg in range(2):
                        for j in range(n):
                            load(u + dg * n + j, kpart(down, row + 2 * j, 2, dg * BANK, (dg + 1) * BANK))
                    row += 2 * n

            sp.dma_start(gains[:, :], w["gains"]).then_inc(s_g, 16)
            load_ffn(0)
            sp.dma_start(bands[:, :, :], w["bands"]).then_inc(s_b, 16)
            for j in range(2):
                load(U0["pool"] + j,
                     w["pool_w"][0, 2 * j:2 * j + 2].rearrange("g (a p) d -> p (g a) d", p=P))
            load_ffn(1)
            sp.dma_start(tab[:, :, :], w["tables"]).then_inc(s_t, 16)
            for j in range(4):
                load(U0["dkv"] + j, kpart(w["w_dkv"], 2 * j, 2, 0, RKV + P))
            load_ffn(2)
            for j in range(3):
                load(U0["dq"] + j, kpart(w["w_dq"][0], 0, KD, j * P, (j + 1) * P))
            load(U0["uk"], kpart(w["w_uk"], 0, KKV, 0, NH * DN))
            load(U0["uv"], kpart(w["w_uv"], 0, KKV, 0, NH * DV))
            for j in range(4):
                load(U0["uq"] + j, kpart(w["w_uq"], 0, KQ, 2 * j * P, 2 * (j + 1) * P))
            for j in range(4):
                load(U0["wo"] + j, kpart(w["w_o"][0], 0, 4, 2 * j * P, 2 * (j + 1) * P))
            load_ffn(3)
            sp.wait_ge(dve_done, at("dve", "ol7"))
            sp.dma_start(heads[0:2 * NH, :], w["heads"]).then_inc(s_h, 16)
            win = w["w_in_2"][0]

            def load_pair(u, c):
                for e in range(2):
                    load(u + e, kpart(win, 4 * e, 4, c, c + 2 * P))

            for e in range(4):
                load_pair(U0["qk"] + 2 * e, SEC["qk"[e // 2]] + 2 * (e % 2) * P)
            for j in range(4):
                load(U0["v"] + j, kpart(win, 2 * j, 2, SEC["v"], SEC["v"] + CW))
            for p in range(2):
                for e, s in enumerate(("cv", "cg")):
                    load_pair(U0["cf"] + 4 * p + 2 * e, SEC[s] + 2 * p * P)
            for p in range(2):
                for e, s in enumerate(("sx", "sc", "sb")):
                    load_pair(U0["sc"] + 6 * p + 2 * e, SEC[s] + 2 * p * P)
            for b, name in enumerate(("w_attn_out_2", "w_conf_out_2", "w_sc_out_2")):
                for p in range(4):
                    u = U0["br"] + (b * 4 + p) * 3
                    load_pair(u, SEC["gate"] + b * D + 2 * p * P)
                    load(u + 2, kpart(w[name][0], 0, CT, 2 * p * P, 2 * (p + 1) * P))
            for p in range(4):
                for e in range(2):
                    load(U0["wo2"] + 2 * p + e, kpart(w["w_o_2"][0], 4 * e, 4, 2 * p * P, 2 * (p + 1) * P))
            load_ffn(4)
            for k in range(KD):
                sp.wait_ge(dve_done, at("dve", f"h:f4out:{k}"))
                sp.dma_start(out[k], x2[:, k, :]).then_inc(s_out, 16)
            sp.wait_ge(s_out, 16 * KD)

        @block.gpsimd
        def _(pool):
            def lo(u, i=0):
                s = u % RING
                pool.wait_ge(h_done, u + 1 + RING * i)
                nc.gpsimd.tensor_tensor(wL[:, s, :], raw[:, s, :], f32(wH[:, s, :]),
                                        ALU.subtract).then_inc(l_done, 1)

            def taps(a, b):
                for tap in range(a, b):
                    wt = gcol("conf_dw_w_2", tap * CT)
                    if tap == 0:
                        pool.wait_ge(dve_done, at("dve", "hb0"))
                        nc.gpsimd.tensor_scalar(conv[:, 0, :], hb[:, 0, 0:SEQ], wt, gcol("conf_dw_b_2", 0),
                                                ALU.mult, ALU.add).then_inc(taps_done, 1)
                    else:
                        pool.wait_ge(taps_done, tap_count(tap - 1))
                        nc.gpsimd.tensor_scalar(tapped, hb[:, 0, tap:tap + SEQ], wt, None,
                                                ALU.mult).then_inc(taps_done, 1)
                        pool.wait_ge(taps_done, tap_count(tap) - 1)
                        nc.gpsimd.tensor_tensor(conv[:, 0, :], tapped, conv[:, 0, :],
                                                ALU.add).then_inc(taps_done, 1)

            u = POOL_FROM // RING * RING
            with pool.Fori(0, u // RING) as i:
                for s in range(RING):
                    lo(s, i)
            while u < POOL_FROM:
                lo(u)
                u += 1
            n = 0
            while n < CONV:
                lo(u)
                taps(n, min(n + POOL_PACE, CONV))
                n, u = n + POOL_PACE, u + 1
            while u % RING:
                lo(u)
                u += 1
            with pool.Fori(0, (NUNITS - u) // RING) as i:
                for s in range(RING):
                    lo(u + s, i)
            for u in range(NUNITS // RING * RING, NUNITS):
                lo(u)

        @block.tensor
        def _(pe):
            owner = [None] * SLOTS
            count = [0]

            def done(ins, name):
                ins.then_inc(pe_done, 1)
                C.tick("pe", name)

            def group(name, reader=None):
                s = count[0] % SLOTS
                count[0] += 1
                if owner[s]:
                    eng, ev, i = owner[s]
                    pe.wait_ge({"dve": dve_done, "act": act_done}[eng], at(eng, ev, i))
                owner[s] = reader or ("dve", "rd:" + name, 0)
                C.slot[name] = s
                return s

            def take(name, last):
                s = count[0] % SLOTS
                count[0] += 1
                owner[s] = ("dve", "rd:" + name, last)
                C.slot[name] = s
                return s

            def product(s, T, wcol, sl, rhs, start, stop):
                aH_, aL_ = rhs
                parts = [(0, HALF), (HALF, T1)] if T == T1 else [(0, T)]
                wh, wl = wH[:, sl, wcol:wcol + P], wL[:, sl, wcol:wcol + P]
                for n, (lhs, r) in enumerate(((wh, aH_), (wh, aL_), (wl, aH_))):
                    for c, (a, b) in enumerate(parts):
                        ins = nc.tensor.matmul(ps[:, 2 * s + c, 0:b - a], lhs, r[:, a:b],
                                               start=start and n == 0, stop=stop and n == 2,
                                               skip_group_check=True)
                return ins

            def weights(u, i=0):
                pe.wait_ge(l_done, u + 1 + RING * i)

            def xs(k, T):
                return xH[:, k, 0:T], xL[:, k, 0:T]

            def stats(name, s, src, lhs, ev):
                pe.wait_ge(dve_done, at("dve", ev))
                for n, ap in enumerate(src):
                    T = ap.shape[1]
                    cuts = [(0, HALF), (HALF, T1)] if T == T1 else [(0, T)]
                    for c, (a, b) in enumerate(cuts):
                        ins = nc.tensor.matmul(ps[:, 2 * s + c, 0:b - a], lhs, ap[:, a:b],
                                               start=n == 0, stop=n == len(src) - 1,
                                               skip_group_check=True)
                done(ins, name)

            def norm_stats(p, T, s):
                stats(f"st:{p}", s, [ss[:, 0:T]], ones, f"ss:{p}:{KD - 1}")

            N_SS = {"kv": KKV, "cq": KQ}

            def borrow(p, T, ahead):
                s = (count[0] + ahead) % SLOTS
                if owner[s]:
                    eng, ev, i = owner[s]
                    pe.wait_ge({"dve": dve_done, "act": act_done}[eng], at(eng, ev, i))
                stats(f"st:{p}", s, [ss[:, 0:T]], ones, f"ss:{p}:{N_SS.get(p, KD) - 1}")
                owner[s] = ("dve", f"rd:st:{p}", 0)
                C.slot[f"st:{p}"] = s

            def ffn(f):
                T = ftok(f)
                for part, n in enumerate(PAIRS):
                    st = f"gu{f}{part}"
                    u = U0[st]

                    def gu(it, i, first):
                        for half, what in enumerate(("gate", "up")):
                            sl = []
                            for e in range(2):
                                uu = u + 2 * half + e
                                weights(uu, i)
                                for j in range(2):
                                    name = f"{st}:{it}:{what}{j}"
                                    if e == 0 and it == "0":
                                        sl.append(group(name))
                                    elif e == 0:
                                        pe.wait_ge(dve_done, at("dve", "rd:" + name, i - 2))
                                        sl.append(take(name, n - 2))
                                    for k in range(4):
                                        if first and half == 0 and j == 0:
                                            pe.wait_ge(dve_done, at("dve", f"xl:f{f}:{4 * e + k}"))
                                        ins = product(sl[j], T, k * 2 * P + j * P, uu % RING,
                                                      xs(4 * e + k, T), e == 0 and k == 0,
                                                      e == 1 and k == 3)
                                    if e == 1 and j == 0:
                                        done(ins, name)
                                done(ins, f"{st}:{it}:u{2 * half + e}" if e == 0 else
                                     f"{st}:{it}:{what}1")
                            if first and half == 0:
                                if f == 0:
                                    pe.wait_ge(s_c, 16)
                                borrow(f"f{f}" if f != 2 else "kv", T, 1)

                    gu("0", 0, part == 0)
                    with pe.Fori(1, n) as i:
                        C.enter("pe", st, i - 1)
                        gu("L", i, False)
                        C.leave("pe", n - 1)
                    st = f"dn{f}{part}"
                    u = U0[st]
                    for dg in range(2):
                        sl = []
                        for js in [(j,) for j in range(n - 2)] + [(n - 2, n - 1)]:
                            for j in js:
                                weights(u + dg * n + j)
                            for d in range(4):
                                if js[0] == 0:
                                    sl.append(group(f"{st}:{4 * dg + d}"))
                                for fl in range(2 * js[0], 2 * js[-1] + 2):
                                    j, e = fl // 2, fl % 2
                                    if dg == 0 and d == 0:
                                        it = ("0", 0) if j == 0 else ("L", j - 1)
                                        pe.wait_ge(dve_done, at("dve", f"gu{f}{part}:{it[0]}:lo{e}", it[1]))
                                    ins = product(sl[d], T, e * 512 + d * P, (u + dg * n + j) % RING,
                                                  (aH[:, fl, 0:T], aL[:, fl, 0:T]),
                                                  fl == 0, fl == 2 * n - 1)
                                if js[-1] == n - 1:
                                    done(ins, f"{st}:{4 * dg + d}")
                            if js[-1] < n - 1:
                                done(ins, f"{st}:u{dg * n + j}")

            def transposed(dst, src, n):
                return nc.tensor.transpose(dst, src, ident[0:n, 0:n])

            ffn(0)

            for j in range(2):
                weights(U0["pool"] + j)
            sl = {}

            def maps(t, gs):
                if t not in sl:
                    sl[t] = group(f"zt:{t}", ("act", f"zt:{t}", 0))
                for g in gs:
                    for a in range(2):
                        k = 2 * g + a
                        if t == 0:
                            pe.wait_ge(dve_done, at("dve", f"xl:pool:{k}"))
                        c = (g % 2 * 2 + a) * 2 * P
                        wh, wl = (x[:, (U0["pool"] + g // 2) % RING, c:c + 2 * P] for x in (wH, wL))
                        xh, xl = (x[:, k, ztok[t]] for x in (xH, xL))
                        for n, (lhs, r) in enumerate(((xh, wh), (xh, wl), (xl, wh))):
                            ins = nc.tensor.matmul(ps[:, 2 * sl[t] + g // 2, g % 2 * 2 * P:(g % 2 + 1) * 2 * P],
                                                   lhs, r, start=a == 0 and n == 0, stop=a == 1 and n == 2,
                                                   skip_group_check=True)
                if g == len(POOL_W) - 1:
                    done(ins, f"zt:{t}")

            last = len(POOL_W) - 1
            for t in range(2):
                maps(t, range(last))
            maps(0, [last])
            s = group("st:pool")
            pe.wait_ge(dve_done, at("dve", f"ss:pool:{KD - 1}"))
            for c in range(NT + 1):
                ins = nc.tensor.matmul(ps[:, 2 * s, c:c + 1], ss[:, ztok[c]], ones[:, 0:1],
                                       start=c == 0, stop=c == NT, skip_group_check=True)
            done(ins, "st:pool")
            maps(1, [last])
            for t in range(2, NT + 1):
                maps(t, range(last + 1))
            pe.wait_ge(s_b, 16)
            for d in range(KD):
                s = group(f"pool:{d}")
                band = bands[:, d // 2, :]
                for t, (o, end) in enumerate(zout):
                    if d == 0:
                        pe.wait_ge(act_done, at("act", f"zt:{t}"))
                    b0 = (P if t else 0) + o - ztok[t].start
                    for lo, hi in ((o, min(end, HALF)), (max(o, HALF), end)):
                        if lo < hi:
                            bank, b = (0, lo) if lo < HALF else (1, lo - HALF)
                            ins = nc.tensor.matmul(ps[:, 2 * s + bank, b:b + hi - lo], zt[:, t, d * P:(d + 1) * P],
                                                   band[:, b0 + lo - o:b0 + hi - o], start=True, stop=True)
                done(ins, f"pool:{d}")

            ffn(1)

            sl = [group(f"dkv:{d}", ("act", f"clat{d}", 0) if d < KKV else None) for d in range(3)]
            for j in range(4):
                weights(U0["dkv"] + j)
                for d in range(3):
                    for a in range(2):
                        k = 2 * j + a
                        if d == 0:
                            pe.wait_ge(dve_done, at("dve", f"xl:dkv:{k}"))
                        ins = product(sl[d], T1, a * (RKV + P) + d * P, (U0["dkv"] + j) % RING, xs(k, T1),
                                      k == 0, k == KD - 1)
                    if j == 3:
                        done(ins, f"dkv:{d}")
                if j < 3:
                    done(ins, f"dkv:u{j}")
            norm_stats("dkv", T1, group("st:dkv"))

            ffn(2)

            for j in range(3):
                s = group(f"dq:{j}")
                weights(U0["dq"] + j)
                for k in range(KD):
                    if j == 0:
                        pe.wait_ge(dve_done, at("dve", f"xl:dq:{k}"))
                    ins = product(s, T1, k * P, (U0["dq"] + j) % RING, xs(k, T1), k == 0, k == KD - 1)
                done(ins, f"dq:{j}")
                if j == 1:
                    borrow("dq", T1, 1)
            weights(U0["uk"])
            for d in range(4):
                s = group(f"uk:{d}", ("act", f"kplain{2 * d + 1}", 0))
                for k in range(KKV):
                    if d == 0:
                        pe.wait_ge(dve_done, at("dve", f"cnl:{k}"))
                    ins = product(s, T1, k * 512 + d * P, U0["uk"] % RING,
                                  (cnH[:, k, :], cnL[:, k, :]), k == 0, k == KKV - 1)
                done(ins, f"uk:{d}")
            stats("st:cq", group("st:cq"), [ss[:, :]], ones, f"ss:cq:{KQ - 1}")
            weights(U0["uv"])
            for t in range(NT + 1):
                s = group(f"uv:{t}")
                a = NMETA + t * P if t < NT else 0
                sl_ = U0["uv"] % RING
                for k in range(KKV):
                    wh, wl = (x[:, sl_, k * 512:(k + 1) * 512] for x in (wH, wL))
                    ch, cl = (x[:, k, a:a + P] for x in (cnH, cnL))
                    for n, (lhs, r) in enumerate(((ch, wh), (ch, wl), (cl, wh))):
                        ins = nc.tensor.matmul(ps[:, 2 * s, :], lhs, r, start=k == 0 and n == 0,
                                               stop=k == KKV - 1 and n == 2, skip_group_check=True)
                done(ins, f"uv:{t}")
            for j in range(4):
                weights(U0["uq"] + j)
                for e in range(2):
                    s = group(f"uq:{2 * j + e}")
                    for k in range(KQ):
                        if j == 0 and e == 0:
                            pe.wait_ge(dve_done, at("dve", f"rd:dq:{k}"))
                        ins = product(s, T1, k * 2 * P + e * P, (U0["uq"] + j) % RING,
                                      (cqH[:, k, :], cqL[:, k, :]), k == 0, k == KQ - 1)
                    done(ins, f"uq:{2 * j + e}")

            s = group("meta:S")
            for hd in range(NH):
                pe.wait_ge(act_done, at("act", f"kcat{hd}"))
                pe.wait_ge(dve_done, at("dve", f"qcat{hd}"))
                ins = nc.tensor.matmul(ps[0:NMETA, 2 * s, hd * NMETA:(hd + 1) * NMETA], qcat[:, hd, 0:NMETA],
                                       kcat[:, hd, 0:NMETA], start=True, stop=True)
            done(ins, "meta:S")

            def meta():
                s = group("meta:T")
                pe.wait_ge(dve_done, at("dve", "meta:p"))
                for hd in range(NH):
                    ins = transposed(ps[0:NMETA, 2 * s, hd * NMETA:(hd + 1) * NMETA], metaP[0:NMETA, 1, hd, :],
                                     NMETA)
                done(ins, "meta:T")

            for what, hd, i in mla_order():
                if (what, hd, i) == ("T", 0, 0):
                    meta()
                s = group(f"mla:{what}{hd}:{i}", {"S": ("act", f"mla:e{hd}:{i}", 0),
                                                  "T": ("act", f"mla:t{hd}:{i}", 0)}.get(what))
                b0, b1 = ps[:, 2 * s, :], ps[:, 2 * s + 1, :]
                if what == "S":
                    q = qcat[:, hd, NMETA + i * P:NMETA + (i + 1) * P]
                    nc.tensor.matmul(b1[:, 0:NMETA], q, kcat[:, hd, 0:NMETA], start=True, stop=True)
                    ins = nc.tensor.matmul(b0[:, BANK - (i + 1) * P:BANK], q,
                                           kcat[:, hd, NMETA:NMETA + (i + 1) * P], start=True, stop=True)
                elif what == "T":
                    pe.wait_ge(dve_done, at("dve", f"mla:p{hd}:{i}"))
                    src = prob[:, (hd * NT + i) % 4, :]
                    w0 = BANK - (i + 1) * P
                    for j in range(i + 1):
                        transposed(b0[:, j * P:(j + 1) * P], src[:, w0 + j * P:w0 + (j + 1) * P], P)
                    ins = transposed(b1[0:NMETA, 0:P], src[:, BANK:BANK + NMETA], P)
                else:
                    pe.wait_ge(act_done, at("act", f"mla:t{hd}:{NT - 1}"))
                    cols = slice(hd // 2 * P, (hd // 2 + 1) * P)
                    for j in range(NT):
                        nc.tensor.matmul(b0[:, j * P:], vreal[:, j, cols], pT[:, hd % 2, j, j * P:],
                                         start=j == 0, stop=False, skip_group_check=True)
                    nc.tensor.matmul(b0[:, :], vmeta[:, cols], pmT[:, hd % 2, :], start=False, stop=True,
                                     skip_group_check=True)
                    if hd == 0:
                        pe.wait_ge(dve_done, at("dve", "rd:meta:T"))
                    ins = nc.tensor.matmul(b1[:, 0:NMETA], vmeta[:, cols], metaT[:, hd * NMETA:(hd + 1) * NMETA],
                                           start=True, stop=True)
                done(ins, f"mla:{what}{hd}:{i}")

            for j in range(4):
                weights(U0["wo"] + j)
                for e in range(2):
                    s = group(f"wo:{2 * j + e}")
                    for k in range(NH // 2):
                        if j == 0 and e == 0:
                            pe.wait_ge(dve_done, at("dve", f"ol{2 * k}"))
                            pe.wait_ge(dve_done, at("dve", f"ol{2 * k + 1}"))
                        ins = product(s, T1, k * 2 * P + e * P, (U0["wo"] + j) % RING,
                                      (oH[:, k, :], oL[:, k, :]), k == 0, k == NH // 2 - 1)
                    done(ins, f"wo:{2 * j + e}")

            ffn(3)

            def quarter(u, stage, n, e, f, kwait=None, ks=range(4)):
                if e == 0:
                    group(f"{stage}:{2 * n + f}")
                if f == 0:
                    weights(u + e)
                s = C.slot[f"{stage}:{2 * n + f}"]
                for k in ks:
                    if kwait and f == 0:
                        pe.wait_ge(dve_done, at("dve", f"xl:{kwait}:{4 * e + k}"))
                    ins = product(s, SEQ, k * 2 * P + f * P, (u + e) % RING, xs(4 * e + k, SEQ),
                                  e == 0 and k == 0, e == 1 and k == 3)
                if 3 not in ks:
                    return
                if e == 1:
                    done(ins, f"{stage}:{2 * n + f}")
                elif f == 1:
                    done(ins, f"{stage}:u{u}")

            def mpair(u, stage, n, kwait=None):
                for e in range(2):
                    for ks in ((range(3), [3]) if kwait and e else (range(4),)):
                        for f in range(2):
                            quarter(u, stage, n, e, f, kwait, ks)

            def head_stats(n):
                for f in range(2 * n, 2 * n + 2):
                    pe.wait_ge(act_done, at("act", f"sq:qk:{f}"))
                    done(nc.tensor.matmul(ps[0:2 * NH, 1, :], hsum[:, f * 2 * NH:(f + 1) * 2 * NH],
                                          sq[:, f % 2, 0:SEQ], start=f == 0, stop=f == NH - 1,
                                          skip_group_check=True), f"st:qk:{f}")

            def head_scales(a, b):
                for f in range(a, b):
                    pe.wait_ge(dve_done, at("dve", "hr" if f < 3 else f"qkn{f - 3}"))
                    done(nc.tensor.matmul(ps[:, f % 3 * 2 + 3, :], heads[0:2 * NH, f * P:(f + 1) * P],
                                          rl[0:2 * NH, 0:SEQ], start=True, stop=True), f"hr:{f}")

            for n in range(4):
                mpair(U0["qk"] + 2 * n, "qk", n, "b2" if n == 0 else None)
                if n == 0:
                    for p, src, ahead in (("final", ss, 0), ("b2", rl, 1)):
                        s = (count[0] + ahead) % SLOTS
                        eng, ev, i = owner[s]
                        pe.wait_ge({"dve": dve_done, "act": act_done}[eng], at(eng, ev, i))
                        stats(f"st:{p}", s, [src[:, 0:SEQ]], ones, f"ss:{p}:{KD - 1}")
                        owner[s] = ("dve", f"rd:st:{p}", 0)
                        C.slot[f"st:{p}"] = s
                else:
                    head_stats(n - 1)
                if n == 2:
                    s = group("rcol")
                    for t in range(NT):
                        ins = nc.tensor.matmul(ps[:, 2 * s, t:t + 1], rs[0:1, t * P:(t + 1) * P],
                                               ones[0:1, 0:1], start=t == 0, stop=t == NT - 1,
                                               skip_group_check=True)
                    done(ins, "rcol")
            head_stats(3)
            sl = [group(f"v:{t}") for t in range(NT)]
            for j in range(4):
                weights(U0["v"] + j)
                for t in range(NT):
                    for a in range(2):
                        k = 2 * j + a
                        wh, wl = (x[:, (U0["v"] + j) % RING, a * 512:(a + 1) * 512] for x in (wH, wL))
                        ch, cl = (x[:, k, t * P:(t + 1) * P] for x in (xH, xL))
                        for n, (lhs, r) in enumerate(((ch, wh), (ch, wl), (cl, wh))):
                            ins = nc.tensor.matmul(ps[:, 2 * sl[t], :], lhs, r, start=k == 0 and n == 0,
                                                   stop=k == KD - 1 and n == 2, skip_group_check=True)
                    if j == 3:
                        done(ins, f"v:{t}")
                if j < 3:
                    done(ins, f"v:u{j}")
                if j == 1:
                    pe.wait_ge(s_h, 16)
                if j:
                    head_scales(3 * j - 3, min(3 * j, NH))

            def logits(hd):
                pe.wait_ge(act_done, at("act", f"qpad{hd}"))
                if hd == 0:
                    pe.wait_ge(dve_done, at("dve", f"qkn{NH - 1}"))
                if hd:
                    pe.wait_ge(dve_done, at("dve", f"rd:o2:{hd - 1}"))
                for j in reversed(range(NT)):
                    b = ps[:, 2 * j + 1, :]
                    n = SEQ - j * P
                    nc.tensor.matmul(b[:, 0:n], k2[:, hd // 2, j * P:(j + 1) * P], qpad[:, j * P:],
                                     start=True, stop=False, skip_group_check=True)
                    done(nc.tensor.matmul(b[:, 0:P], maskR[:, 0, :], maskR[:, 1, :], start=False, stop=False,
                                          skip_group_check=True), f"z{hd}:{j}")

            def sums(hd):
                for j in reversed(range(NT)):
                    b = ps[:, 2 * j + 1, :]
                    pe.wait_ge(dve_done, at("dve", f"sp{hd}:{j}"))
                    ins = nc.tensor.matmul(b[:, 0:SEQ - j * P], ntri, spl(j), start=False, stop=j == NT - 1,
                                           skip_group_check=True)
                    if later(j):
                        pe.wait_ge(dve_done, at("dve", f"later{hd}:{j}"))
                    for o, t in later(j):
                        ins = nc.tensor.matmul(b[:, o:o + t.shape[-1]], none_, t, start=False,
                                               stop=o + t.shape[-1] == SEQ - j * P, skip_group_check=True)
                    done(ins, f"r{hd}:{j}")

            def values(hd):
                b = ps[:, 2 * NT - 1, :]
                for j in reversed(range(NT)):
                    pe.wait_ge(act_done, at("act", f"a{hd}:{j}"))
                    ins = nc.tensor.matmul(b[:, j * P:], v2[:, j, hd // 2 * P:(hd // 2 + 1) * P], attn(j),
                                           start=j == NT - 1, stop=j == 0, skip_group_check=True)
                done(ins, f"o2:{hd}")

            for what, *at_ in blend_order():
                if what == "z":
                    logits(*at_)
                elif what == "r":
                    sums(*at_)
                elif what == "o":
                    values(*at_)
                else:
                    n, e, f = at_
                    quarter(U0[what] + 2 * n, what, n, e, f)

            inner = ((o2H, o2L), (hbH, hbL), (hcH, hcL))
            ready = ("o2l", "hbl", "hcl")
            for b in range(3):
                for p in range(4):
                    u = U0["br"] + (b * 4 + p) * 3
                    mpair(u, f"gate{b}", p)
                    weights(u + 2)
                    for e in range(2):
                        s = group(f"y{b}:{2 * p + e}")
                        for k in range(CT):
                            if p == 0 and e == 0:
                                pe.wait_ge(dve_done, at("dve", f"{ready[b]}{k}"))
                            ins = product(s, SEQ, k * 2 * P + e * P, (u + 2) % RING,
                                          (inner[b][0][:, k, :], inner[b][1][:, k, :]),
                                          k == 0, k == CT - 1)
                        done(ins, f"y{b}:{2 * p + e}")
                    if b == 0 and p == 0:
                        pe.wait_ge(taps_done, tap_count(CONV - 1))
                        stats("st:mean", group("st:mean"), [conv[:, c, :] for c in range(CT)], ones,
                              f"conv{CONV - 1}:{CT - 1}")
                    if b == 0 and p == 1:
                        stats("st:lnv", group("st:lnv"), [ss[:, 0:SEQ]], ones, f"ss:ln:{CT - 1}")
            for p in range(4):
                u = U0["wo2"] + 2 * p
                sl = [group(f"wo2:{2 * p}"), group(f"wo2:{2 * p + 1}")]
                for e in range(2):
                    weights(u + e)
                    for f in range(2):
                        for k in range(4):
                            if p == 0 and f == 0:
                                pe.wait_ge(dve_done, at("dve", f"mgl{4 * e + k}"))
                            ins = product(sl[f], SEQ, k * 2 * P + f * P, (u + e) % RING,
                                          (mgH[:, 4 * e + k, :], mgL[:, 4 * e + k, :]),
                                          e == 0 and k == 0, e == 1 and k == 3)
                        if e == 1 and f == 0:
                            done(ins, f"wo2:{2 * p}")
                    done(ins, f"wo2:{2 * p + 1}" if e else f"wo2:u{u}")
            ffn(4)

        @block.scalar
        def _(act):
            def fn(ins, *names):
                ins.then_inc(act_done, 1)
                C.tick("act", *names)

            def on_dve(name, i=0):
                act.wait_ge(dve_done, at("dve", name, i))

            def on_pe(name, i=0):
                act.wait_ge(pe_done, at("pe", name, i))

            def split(u, i=0, name=None, ix=0):
                if u >= NUNITS:
                    return
                if name:
                    on_pe(name, ix)
                act.wait_ge(raw_in[u % RING], RAW_AT[u] + 16 * i)
                nc.scalar.activation(wH[:, u % RING, :], raw[:, u % RING, :], ACT.Copy)\
                    .then_inc(h_done, 1)

            def after(stage, j, name):
                split(U0[stage] + j + RING, 0, name)

            def src(p, k):
                return x2[:, k, :] if p in ("b2", "f4") else h[:, k, :]

            def prep(p, k, gain, T, squares=True):
                if p != "f0":
                    on_dve(f"h:{p}:{k}")
                if squares:
                    if k >= 2:
                        on_dve(f"ss:{p}:{k - 2}")
                    fn(nc.scalar.activation(sq[:, k % 2, 0:T], src(p, k), ACT.Square), f"sq:{p}:{k}")
                if gain:
                    fn(nc.scalar.activation(xH[:, k, 0:T], src(p, k), ACT.Copy, scale=gcol(*gain, k)),
                       f"xh:{p}:{k}")

            def prep_blocks(k):
                on_dve(f"h:final:{k}")
                if k >= 2:
                    on_dve(f"ss:b2:{k - 2}")
                fn(nc.scalar.activation(sq[:, k % 2, 0:SEQ], x2[:, k, :], ACT.Square))
                fn(nc.scalar.activation(t2[:, k % 2, 0:SEQ], x2[:, k, :], ACT.Square,
                                        scale=gcol("final_norm", k)), f"sq:final:{k}")
                fn(nc.scalar.activation(xH[:, k, 0:SEQ], x2[:, k, :], ACT.Copy, scale=gcol("block2", k)),
                   f"xh:b2:{k}")

            def root(p, T):
                on_dve(f"rd:st:{p}")
                fn(nc.scalar.activation(sd[:, 0:T], var[:, 0:T], ACT.Abs_reciprocal_sqrt), f"sd:{p}")

            def ffn(f, p=None, gain=None):
                T = ftok(f)
                if f != 2:
                    root(f"f{f}", T)
                for part, n in enumerate(PAIRS):
                    st = f"gu{f}{part}"
                    u = U0[st] + RING

                    def gu(it, i, ix):
                        for half, names in enumerate((("u0", "gate1"), ("u2", "up1"))):
                            for e in range(2):
                                split(u + 2 * half + e, i, f"{st}:{it}:{names[e]}", ix)
                            for j in range(2):
                                if half == 0:
                                    on_dve(f"{st}:{it}:g{j}", ix)
                                    fn(nc.scalar.activation(t2[:, j, 0:T], t1[:, j, 0:T], ACT.Silu),
                                       f"{st}:{it}:silu{j}")
                                else:
                                    on_dve(f"rd:{st}:{it}:up{j}", ix)
                                    fn(nc.scalar.activation(
                                        aH[:, bass.ds(2 * i + j, 1), 0:T] if it == "L" else aH[:, j:j + 1, 0:T],
                                        m[:, j:j + 1, 0:T], ACT.Copy), f"{st}:{it}:ah{j}")

                    gu("0", 0, 0)
                    with act.Fori(1, n) as i:
                        C.enter("act", st, i - 1)
                        gu("L", i, i - 1)
                        C.leave("act", n - 1)
                    st = f"dn{f}{part}"
                    for dg in range(2):
                        for j in range(n - 2):
                            after(st, dg * n + j, f"{st}:u{dg * n + j}")
                        if part == 1 and p:
                            for k in range(4 * dg, 4 * dg + 4):
                                (prep_blocks(k) if p == "final" else prep(p, k, gain, T))
                        for j in range(n - 2, n):
                            after(st, dg * n + j, f"{st}:{4 * dg + 3}")

            act.wait_ge(s_g, 16)
            fn(nc.scalar.activation(gcol("q_norm_g_2", 0), gcol("q_norm_g_2", 0), ACT.Copy, scale=1 / np.sqrt(DV)),
               "q_gain")
            for k, what in first_order():
                if what == "square":
                    prep("f0", k, None, T1)
                elif k % 2:
                    prep("f0", k, ("ffn1_norm",), T1, squares=False)
                else:
                    if k % 4 == 0:
                        split(k // 4)
                    act.wait_ge(s_x[k // 2], 16)
                    prep("f0", k, ("ffn1_norm",), T1, squares=False)
            split(2)
            split(3)
            ffn(0, "pool", ("mix_norm",))
            on_dve("rd:st:pool")
            fn(nc.scalar.activation(psd, pvar, ACT.Abs_reciprocal_sqrt), "sd:pool")
            on_dve("rs:pool")
            for t in range(NT + 1):
                on_pe(f"zt:{t}")
                fn(nc.scalar.activation(zt[:, t, :], flat(C.slot.get(f"zt:{t}", 0)), ACT.Copy,
                                        scale=prs[:, t:t + 1]), f"zt:{t}")
            for k in range(KD):
                prep("f1", k, ("ffn2_norm",), T1)
                if k < 2:
                    after("pool", k, f"zt:{NT}")
            ffn(1, "dkv", ("kv_in_norm",))

            def again(j):
                on_pe(f"dkv:u{j}" if j < 3 else "dkv:2")
                for k in (2 * j, 2 * j + 1):
                    fn(nc.scalar.activation(xH[:, k, :], h[:, k, :], ACT.Copy,
                                            scale=gcol("ffn1_norm", KD + k)), f"xh:f2:{k}")

            for j in range(3):
                after("dkv", j, f"dkv:u{j}")
                again(j)
            for d in range(KKV):
                on_pe(f"dkv:{d}")
                fn(nc.scalar.activation(pairs(clat[:, d, :]), slot(f"dkv:{d}", T1), ACT.Copy), f"clat{d}")
            again(3)
            root("dkv", T1)
            after("dkv", 3, "dkv:2")
            for k in range(KKV):
                on_dve("ss:dkv:7")
                act.wait_ge(act_done, at("act", f"clat{k}"))
                fn(nc.scalar.activation(sq[:, k, :], clat[:, k, :], ACT.Square), f"sq:kv:{k}")
            on_dve("var:kv")
            fn(nc.scalar.activation(sd[:, :], var[:, :], ACT.Abs_reciprocal_sqrt), "sd:kv")
            ffn(2, "dq", ("mix_norm1",))

            for k in range(KKV):
                fn(nc.scalar.activation(cnH[:, k, :], clat[:, k, :], ACT.Copy), f"cnh:{k}")
            for k in range(KQ):
                after("dq", k, f"dq:{k}")
                on_dve(f"ss:dq:{KD - 1}" if k < 2 else "ss:cq:0")
                fn(nc.scalar.activation(pairs(sq[:, k % 2, :]), slot(f"dq:{k}", T1), ACT.Square), f"sq:cq:{k}")
                fn(nc.scalar.activation(pairs(cqH[:, k, :]), slot(f"dq:{k}", T1), ACT.Copy,
                                        scale=gcol("q_latent_norm", k)), f"cqh:{k}")
                if k == 1:
                    root("dq", T1)
            for hd in range(NH):
                on_pe(f"uk:{hd // 2}")
                r = hd % 2 * DN
                fn(nc.scalar.activation(pairs(kcat[0:DN, hd, :]), slot(f"uk:{hd // 2}", T1)[r:r + DN],
                                        ACT.Copy), f"kplain{hd}")
            after("uk", 0, "uk:3")
            on_dve("var:cq")
            fn(nc.scalar.activation(sd[:, :], var[:, :], ACT.Abs_reciprocal_sqrt), "sd:cq")
            for hd in range(NH):
                fn(nc.scalar.activation(kcat[DN:P, hd, :], krope[DN:P, :], ACT.Copy), f"kcat{hd}")
            after("uv", 0, "uv:4")
            for j in range(4):
                after("uq", j, f"uq:{2 * j + 1}")
            on_dve("meta:d")
            fn(nc.scalar.activation(metaP[0:NMETA, 1], metaP[0:NMETA, 0], ACT.Exp), "meta:e")
            for what, hd, i in mla_order():
                s = C.slot.get(f"mla:{what}{hd}:{i}", 0)
                lo = BANK - (i + 1) * P
                st = (hd * NT + i) % 2
                if what == "S":
                    on_dve(f"mla:m{hd}:{i}")
                    fn(nc.scalar.activation(t2[:, st, lo:T1], flat(s)[:, lo:T1], ACT.Exp,
                                            bias=small[:, 4 * st:4 * st + 1],
                                            accum_out=small[:, 4 * st + 1:4 * st + 2]), f"mla:e{hd}:{i}")
                elif what == "T":
                    on_pe(f"mla:T{hd}:{i}")
                    if hd >= 2:
                        on_pe(f"mla:V{hd - 2}:0")
                    fn(nc.scalar.activation(pT[:, hd % 2, 0:i + 1, i * P:(i + 1) * P],
                                            ps[:, 2 * s, 0:(i + 1) * P].rearrange("p (j q) -> p j q", j=i + 1),
                                            ACT.Copy))
                    fn(nc.scalar.activation(pmT[0:NMETA, hd % 2, i * P:(i + 1) * P], ps[0:NMETA, 2 * s + 1, 0:P],
                                            ACT.Copy), f"mla:t{hd}:{i}")
                else:
                    on_pe(f"mla:V{hd}:{i}")
                    r = slice(hd % 2 * DV, hd % 2 * DV + DV)
                    fn(nc.scalar.activation(oH[r, hd // 2, NMETA:], ps[r, 2 * s, :], ACT.Copy))
                    fn(nc.scalar.activation(oH[r, hd // 2, 0:NMETA], ps[r, 2 * s + 1, 0:NMETA],
                                            ACT.Copy), f"oh{hd}")
            for j in range(4):
                after("wo", j, f"wo:{2 * j + 1}")
                for d in (2 * j, 2 * j + 1):
                    prep("f3", d, ("ffn2_norm1",), T1)
            ffn(3, "final")

            for n in range(4):
                after("qk", 2 * n, f"qk:u{U0['qk'] + 2 * n}")
                after("qk", 2 * n + 1, f"qk:{2 * n + 1}")
                if n == 0:
                    root("final", SEQ)
                    on_dve("var:b2")
                    fn(nc.scalar.activation(sd[:, 0:SEQ], var[:, 0:SEQ], ACT.Abs_reciprocal_sqrt), "sd:b2")
                for f in (2 * n, 2 * n + 1):
                    on_dve(f"rd:qk:{f}")
                    if f >= 2:
                        on_pe(f"st:qk:{f - 2}")
                    fn(nc.scalar.activation(sq[:, f % 2, 0:SEQ], (q2, k2)[f // 4][:, f % 4, :], ACT.Square),
                       f"sq:qk:{f}")
            on_dve("var:qk")
            fn(nc.scalar.activation(sd[0:2 * NH, 0:SEQ], var[0:2 * NH, 0:SEQ], ACT.Abs_reciprocal_sqrt), "sd:qk")
            for j in range(4):
                after("v", j, f"v:u{j}" if j < 3 else "v:3")

            def query(hd):
                on_dve(f"qz{hd}")
                if hd == 0:
                    fn(nc.scalar.activation(maskR[:, 0, :], ident, ACT.Copy))
                    fn(nc.scalar.activation(maskR[:, 1, :], mask, ACT.Copy))
                r = slice(hd % 2 * DV, hd % 2 * DV + DV)
                fn(nc.scalar.activation(qpad[r, :], q2[r, hd // 2, :], ACT.Copy), f"qpad{hd}")

            def softplus(hd):
                for j in reversed(range(NT)):
                    on_pe(f"z{hd}:{j}")
                    fn(nc.scalar.activation(spl(j), ps[:, 2 * j + 1, 0:SEQ - j * P], ACT.Abs), f"abs{hd}:{j}")
                for j in reversed(range(NT)):
                    act.wait_ge(act_done, at("act", f"abs{hd}:{j}"))
                    fn(nc.scalar.activation(spl(j), spl(j), ACT.Exp, scale=-1.0), f"exp{hd}:{j}")
                for j in reversed(range(NT)):
                    act.wait_ge(act_done, at("act", f"exp{hd}:{j}"))
                    fn(nc.scalar.activation(spl(j), spl(j), ACT.Ln, bias=ones[:, 0:1]), f"ln{hd}:{j}")

            query(0)
            behind = None
            for what, *at_ in blend_order() + [("end",)]:
                if what == "z":
                    softplus(*at_)
                elif what == "r":
                    hd, = at_
                    for j in reversed(range(NT)):
                        on_pe(f"r{hd}:{j}")
                        fn(nc.scalar.activation(attn(j), ps[:, 2 * j + 1, 0:SEQ - j * P], ACT.Exp), f"a{hd}:{j}")
                elif what == "o":
                    hd, = at_
                    if hd + 1 < NH:
                        query(hd + 1)
                    if hd % 2:
                        on_dve(f"rd:o2:{hd}")
                        fn(nc.scalar.activation(o2H[:, hd // 2, :], o2[:, hd // 2, :], ACT.Copy), f"o2h{hd // 2}")
                if behind is not None:
                    for x in (behind, behind + 1):
                        on_dve(f"rd:cf:{x}")
                        fn(nc.scalar.activation(m[:, x % 2, 0:SEQ], t2[:, x % 2, 0:SEQ], ACT.Sigmoid), f"sig:cf:{x}")
                    behind = None
                if what in ("cf", "sc"):
                    n, e, f = at_
                    if f == 1:
                        after(what, 2 * n + e, f"{what}:{2 * n + 1}" if e else f"{what}:u{U0[what] + 2 * n}")
                    if what == "cf" and n % 2 and e == f == 1:
                        behind = 2 * n

            def layer_norm(p):
                if p == 1:
                    for c in range(CT):
                        on_dve(f"cm:{c}")
                        if c >= 2:
                            on_dve(f"ss:ln:{c - 2}")
                        fn(nc.scalar.activation(sq[:, c % 2, 0:SEQ], conv[:, c, :], ACT.Square), f"sq:ln:{c}")
                elif p == 2:
                    on_dve("rd:st:lnv")
                    fn(nc.scalar.activation(sd[:, 0:SEQ], var[:, 0:SEQ], ACT.Abs_reciprocal_sqrt), "sd:ln")
                elif p == 3:
                    for c in range(CT):
                        on_dve(f"ln:{c}")
                        fn(nc.scalar.activation(hbn[:, c % 2, 0:SEQ], lnt[:, c % 2, 0:SEQ], ACT.Silu,
                                                bias=gcol("conf_ln_b_2", c), scale=gcol("conf_ln_g_2", c)),
                           f"hbn{c}")
                        act.wait_ge(act_done, at("act", f"hbn{c}"))
                        fn(nc.scalar.activation(hbH[:, c, :], hbn[:, c % 2, 0:SEQ], ACT.Copy), f"hbh{c}")
                        fn(nc.scalar.activation(hcH[:, c, :], hcr[:, c, :], ACT.Copy), f"hch{c}")

            for b in range(3):
                for p in range(4):
                    j = (b * 4 + p) * 3
                    after("br", j, f"gate{b}:u{U0['br'] + j}")
                    after("br", j + 1, f"gate{b}:{2 * p + 1}")
                    for e in range(2):
                        d = 2 * p + e
                        on_dve(f"rd:gate{b}:{d}")
                        fn(nc.scalar.activation(t2[:, e, 0:SEQ], t1[:, e, 0:SEQ], ACT.Sigmoid,
                                                bias=gcol("gate_b_2", b * KD + d)), f"sig{b}:{d}")
                    after("br", j + 2, f"y{b}:{2 * p + 1}")
                    if b == 2:
                        for d in (2 * p, 2 * p + 1):
                            on_dve(f"mg:{d}")
                            fn(nc.scalar.activation(mgH[:, d, :], merged[:, d, :], ACT.Copy), f"mgh:{d}")
                    if b == 0:
                        layer_norm(p + 1)
            for p in range(4):
                after("wo2", 2 * p, f"wo2:u{U0['wo2'] + 2 * p}")
                after("wo2", 2 * p + 1, f"wo2:{2 * p + 1}")
                for d in (2 * p, 2 * p + 1):
                    prep("f4", d, ("ffn_norm_g_2",), SEQ)
            ffn(4)

        @block.vector
        def _(dve):
            V = nc.vector

            def do(ins, *names):
                ins.then_inc(dve_done, 1)
                C.tick("dve", *names)

            def own(name=None):
                dve.wait_ge(dve_done, at("dve", name) if name else C.here("dve"))

            def on_act(name, i=0):
                dve.wait_ge(act_done, at("act", name, i))

            def on_pe(name, i=0):
                dve.wait_ge(pe_done, at("pe", name, i))

            def src(p, k):
                return x2[:, k, :] if p in ("b2", "f4") else h[:, k, :]

            def prep(p, k, gain, T, squares=True):
                if squares:
                    on_act(f"sq:{p}:{k}")
                    if k == 0:
                        do(V.tensor_copy(ss[:, 0:T], sq[:, 0, 0:T]), f"ss:{p}:0")
                    else:
                        own(f"ss:{p}:{k - 1}")
                        do(V.tensor_tensor(ss[:, 0:T], ss[:, 0:T], sq[:, k % 2, 0:T], ALU.add), f"ss:{p}:{k}")
                if gain:
                    on_act(f"xh:{p}:{k}")
                    do(V.scalar_tensor_tensor(xL[:, k, 0:T], src(p, k), gcol(*gain, k), f32(xH[:, k, 0:T]),
                                              ALU.mult, ALU.subtract), f"xl:{p}:{k}")

            def prep_blocks(k):
                on_act(f"sq:final:{k}")
                own()
                for p, total, square in (("final", ss, sq), ("b2", rl, t2)):
                    if k == 0:
                        do(V.tensor_copy(total[:, 0:SEQ], square[:, 0, 0:SEQ]), f"ss:{p}:0")
                    else:
                        do(V.tensor_tensor(total[:, 0:SEQ], total[:, 0:SEQ], square[:, k % 2, 0:SEQ], ALU.add),
                           f"ss:{p}:{k}")
                on_act(f"xh:b2:{k}")
                do(V.scalar_tensor_tensor(xL[:, k, 0:SEQ], x2[:, k, :], gcol("block2", k), f32(xH[:, k, 0:SEQ]),
                                          ALU.mult, ALU.subtract), f"xl:b2:{k}")

            def variance(p, T, n):
                on_pe(f"st:{p}")
                own()
                do(V.tensor_scalar(like(var[:, 0:T], T), slot(f"st:{p}", T), 1.0 / n, EPS, ALU.mult, ALU.add),
                   f"rd:st:{p}")

            def rsqrt(r, v, s, root):
                on_act(root)
                own()
                do(V.tensor_tensor(r, s, s, ALU.mult))
                own()
                do(V.scalar_tensor_tensor(r, r, -0.5, v, ALU.mult, ALU.mult))
                own()
                do(V.scalar_tensor_tensor(r, r, 1.5, s, ALU.add, ALU.mult))

            def scales(p, T, n=D, r=rs):
                variance(p, T, n)
                rsqrt(r[:, 0:T], var[:, 0:T], sd[:, 0:T], f"sd:{p}")
                own()

            def scaled(out, name, T, *names):
                on_pe(name)
                do(V.tensor_tensor(like(out, T), slot(name, T), like(rs[:, 0:T], T), ALU.mult),
                   "rd:" + name, *names)

            def ffn(f, p=None, gain=None):
                T = ftok(f)
                if f != 2:
                    scales(f"f{f}", T)
                for part, n in enumerate(PAIRS):
                    st = f"gu{f}{part}"

                    def gu(it, i, ix):
                        for j in range(2):
                            name = f"{st}:{it}:gate{j}"
                            on_pe(name, ix)
                            do(V.tensor_tensor(like(t1[:, j, 0:T], T), slot(name, T), like(rs[:, 0:T], T),
                                               ALU.mult), "rd:" + name, f"{st}:{it}:g{j}")
                        for j in range(2):
                            name = f"{st}:{it}:up{j}"
                            on_pe(name, ix)
                            on_act(f"{st}:{it}:silu{j}", ix)
                            own()
                            do(V.tensor_tensor(like(m[:, j, 0:T], T), slot(name, T), like(t2[:, j, 0:T], T),
                                               ALU.mult), "rd:" + name)
                        for j in range(2):
                            on_act(f"{st}:{it}:ah{j}", ix)
                            fl = bass.ds(2 * i + j, 1) if it == "L" else slice(j, j + 1)
                            do(V.tensor_tensor(aL[:, fl, 0:T], m[:, j:j + 1, 0:T], f32(aH[:, fl, 0:T]),
                                               ALU.subtract), f"{st}:{it}:lo{j}")

                    gu("0", 0, 0)
                    with dve.Fori(1, n) as i:
                        C.enter("dve", st, i - 1)
                        gu("L", i, i - 1)
                        C.leave("dve", n - 1)
                    last = part == 1
                    for d in range(KD):
                        name = f"dn{f}{part}:{d}"
                        on_pe(name)
                        own()
                        do(V.scalar_tensor_tensor(like(m[:, d % 2, 0:T], T), slot(name, T),
                                                  0.5 if f < 4 else 1.0, like(rs[:, 0:T], T),
                                                  ALU.mult, ALU.mult), "rd:" + name)
                        own()
                        hd = x2[:, d, :] if f == 4 else h[:, d, :]
                        do(V.tensor_tensor(hd, hd, m[:, d % 2, 0:T], ALU.add),
                           *([f"h:{p or 'f4out'}:{d}"] if last else []))
                        if last and p and d:
                            (prep_blocks(d - 1) if p == "final" else prep(p, d - 1, gain, T))
                    if last and p:
                        (prep_blocks(KD - 1) if p == "final" else prep(p, KD - 1, gain, T))

            dve.wait_ge(s_g, 16)
            cols = {n: gains[:, GAIN[n][0]:GAIN[n][0] + KD] for n in ("final_norm", "mix_norm_g_2")}
            do(V.tensor_tensor(gblk[:, :], cols["final_norm"], cols["mix_norm_g_2"], ALU.mult), "gblk")
            for k, what in first_order():
                prep("f0", k, None if what == "square" else ("ffn1_norm",), T1, squares=what == "square")
            ffn(0, "pool", ("mix_norm",))

            on_pe("st:pool")
            do(V.tensor_scalar(pvar, slot("st:pool", SEQ)[:, 0:NT + 1], 1.0 / D, EPS, ALU.mult, ALU.add), "rd:st:pool")
            rsqrt(prs, pvar, psd, "sd:pool")
            C.also("dve", "rs:pool")
            for d in range(KD):
                on_pe(f"pool:{d}")
                do(V.scalar_tensor_tensor(pairs(h[:, d, :]), slot(f"pool:{d}", T1), gcol("pool_scale", d),
                                          pairs(h[:, d, :]), ALU.mult, ALU.add), f"rd:pool:{d}", f"h:f1:{d}")
                if d:
                    prep("f1", d - 1, ("ffn2_norm",), T1)
            prep("f1", KD - 1, ("ffn2_norm",), T1)
            ffn(1, "dkv", ("kv_in_norm",))

            for k in range(6):
                prep("f2", k, ("ffn1_norm1",), T1, squares=False)
            variance("dkv", T1, D)
            dve.wait_ge(s_t, 16)
            on_pe("dkv:2")
            upper, rope = slice(DN, P), slot("dkv:2", T1)
            do(V.tensor_tensor(pairs(m[upper, 0, :]), rope[0:DN], pairs(tab[0:DN, TAB_COS, :]), ALU.mult))
            do(V.tensor_tensor(pairs(m[upper, 1, :]), rope[upper], pairs(tab[upper, TAB_SIN, :]), ALU.mult),
               "rd:dkv:2")
            for k in range(6, KD):
                prep("f2", k, ("ffn1_norm1",), T1, squares=False)
            rsqrt(rs[:, :], var[:, :], sd[:, :], "sd:dkv")

            def add_square(p, k, T):
                on_act(f"sq:{p}:{k}")
                own()
                if k == 0:
                    do(V.tensor_copy(ss[:, 0:T], sq[:, 0, 0:T]), f"ss:{p}:0")
                else:
                    do(V.tensor_tensor(ss[:, 0:T], ss[:, 0:T], sq[:, k % 2, 0:T], ALU.add), f"ss:{p}:{k}")

            own()
            do(V.tensor_tensor(m[upper, 0, :], m[upper, 0, :], m[upper, 1, :], ALU.add))
            own()
            do(V.tensor_tensor(krope[upper, :], m[upper, 0, :], rs[upper, :], ALU.mult), "krope")
            for k in range(KKV):
                add_square("kv", k, T1)
            def latent_scales(p, n):
                do(V.tensor_tensor(rl[:, :], rs[:, :], rs[:, :], ALU.mult))
                on_pe(f"st:{p}")
                own()
                do(V.scalar_tensor_tensor(pairs(var[:, :]), slot(f"st:{p}", T1), 1.0 / n, pairs(rl[:, :]),
                                          ALU.mult, ALU.mult), f"rd:st:{p}")
                own()
                do(V.tensor_scalar(var[:, :], var[:, :], EPS, None, ALU.add), f"var:{p}")

            def latent_rsqrt(p):
                rsqrt(rl[:, :], var[:, :], sd[:, :], f"sd:{p}")
                own()
                do(V.tensor_tensor(rl[:, :], rl[:, :], rs[:, :], ALU.mult))

            latent_scales("kv", RKV)
            latent_rsqrt("kv")
            own()
            for k in range(KKV):
                do(V.scalar_tensor_tensor(clat[:, k, :], clat[:, k, :], gcol("kv_latent_norm", k), rl[:, :],
                                          ALU.mult, ALU.mult), f"cn:{k}")
            ffn(2, "dq", ("mix_norm1",))

            for k in range(KKV):
                on_act(f"cnh:{k}")
                do(V.tensor_tensor(cnL[:, k, :], clat[:, k, :], f32(cnH[:, k, :]), ALU.subtract), f"cnl:{k}")
            for k in range(KQ):
                if k == 2:
                    scales("dq", T1)
                    add_square("cq", 0, T1)
                    add_square("cq", 1, T1)
                on_act(f"cqh:{k}")
                do(V.scalar_tensor_tensor(pairs(cqL[:, k, :]), slot(f"dq:{k}", T1), gcol("q_latent_norm", k),
                                          pairs(f32(cqH[:, k, :])), ALU.mult, ALU.subtract), f"rd:dq:{k}")
            add_square("cq", 2, T1)
            latent_scales("cq", RQ)
            do(V.memset(vmeta[:, :], 0.0))
            do(V.memset(pmT[:, :, :], 0.0))
            do(V.memset(metaT[:, :], 0.0))
            own()
            for t in range(NT + 1):
                on_pe(f"uv:{t}")
                if t < NT:
                    do(V.tensor_copy(vreal[:, t, :], slot(f"uv:{t}", SEQ)), f"rd:uv:{t}")
                else:
                    do(V.tensor_copy(vmeta[0:NMETA, :], slot(f"uv:{t}", SEQ)[0:NMETA]), f"rd:uv:{t}")
                if t == 1:
                    latent_rsqrt("cq")
                    own()
                    do(V.tensor_tensor(ss[:, :], tab[:, TAB_Q, :], rl[:, :], ALU.mult))
            own()
            for hd in range(NH):
                on_pe(f"uq:{hd}")
                do(V.tensor_tensor(pairs(qcat[:, hd, :]), slot(f"uq:{hd}", T1), pairs(ss[:, :]), ALU.mult),
                   f"rd:uq:{hd}", f"qcat{hd}")

            mmax, msum, mrec = (small[0:NMETA, 16 + i * NH:16 + (i + 1) * NH] for i in range(3))

            def per_head(ap):
                return ap.unsqueeze(2).broadcast_to([NMETA, NH, NMETA])

            on_pe("meta:S")
            scores = slot("meta:S", SEQ)[0:NMETA, 0:NH * NMETA].rearrange("p (h k) -> p h k", h=NH)
            do(V.tensor_reduce(mmax, scores, AX_X, ALU.max))
            own()
            do(V.tensor_tensor(metaP[0:NMETA, 0], scores, per_head(mmax), ALU.subtract), "rd:meta:S", "meta:d")

            def meta():
                on_act("meta:e")
                do(V.tensor_reduce(msum, metaP[0:NMETA, 1], AX_X, ALU.add))
                own()
                do(V.reciprocal(mrec, msum))
                own()
                do(V.tensor_tensor(metaP[0:NMETA, 1], metaP[0:NMETA, 1], per_head(mrec), ALU.mult), "meta:p")

            order = mla_order()
            steps = [(hd, i) for what, hd, i in order if what == "S"]

            def normalise(n):
                hd, i = steps[n]
                lo = BANK - (i + 1) * P
                rec = small[:, 4 * (n % 2) + 2:4 * (n % 2) + 3]
                on_act(f"mla:e{hd}:{i}")
                do(V.reciprocal(rec, small[:, 4 * (n % 2) + 1:4 * (n % 2) + 2]))
                if n >= 4:
                    on_pe(f"mla:T{steps[n - 4][0]}:{steps[n - 4][1]}")
                own()
                do(V.tensor_scalar(prob[:, n % 4, lo:T1], t2[:, n % 2, lo:T1], rec, None, ALU.mult),
                   f"mla:p{hd}:{i}")

            for what, hd, i in order:
                s = C.slot.get(f"mla:{what}{hd}:{i}", 0)
                n = hd * NT + i
                if what == "S":
                    lo = BANK - (i + 1) * P
                    on_pe(f"mla:S{hd}:{i}")
                    do(V.memset(flat(s)[0:P // 2, BANK - P // 2:BANK], NEG))
                    own()
                    do(V.tensor_reduce(small[:, 4 * (n % 2):4 * (n % 2) + 1], flat(s)[:, lo:T1], AX_X, ALU.max,
                                       negate=True), f"mla:m{hd}:{i}")
                    if n:
                        normalise(n - 1)
                    if n == 1:
                        meta()
                elif what == "T":
                    if (hd, i) == steps[-3]:
                        normalise(len(steps) - 1)
                    if (hd, i) == steps[0]:
                        on_pe("meta:T")
                        do(V.tensor_copy(metaT[0:NMETA, :], slot("meta:T", SEQ)[0:NMETA, 0:NH * NMETA]), "rd:meta:T")
                else:
                    on_act(f"oh{hd}")
                    r = slice(hd % 2 * DV, hd % 2 * DV + DV)
                    do(V.tensor_tensor(oL[r, hd // 2, NMETA:], ps[r, 2 * s, :], f32(oH[r, hd // 2, NMETA:]),
                                       ALU.subtract))
                    do(V.tensor_tensor(oL[r, hd // 2, 0:NMETA], ps[r, 2 * s + 1, 0:NMETA],
                                       f32(oH[r, hd // 2, 0:NMETA]), ALU.subtract),
                       f"ol{hd}", f"rd:mla:V{hd}:0")
            for d in range(KD):
                on_pe(f"wo:{d}")
                own()
                do(V.tensor_tensor(pairs(h[:, d, :]), slot(f"wo:{d}", T1), pairs(h[:, d, :]), ALU.add),
                   f"rd:wo:{d}", f"h:f3:{d}")
                if d:
                    prep("f3", d - 1, ("ffn2_norm1",), T1)
            prep("f3", KD - 1, ("ffn2_norm1",), T1)
            ffn(3, "final")

            variance("final", SEQ, D)
            on_pe("st:b2")
            do(V.tensor_scalar(m[:, 0, 0:SEQ], slot("st:b2", SEQ), 1.0 / D, None, ALU.mult), "rd:st:b2")
            rsqrt(ss[:, 0:SEQ], var[:, 0:SEQ], sd[:, 0:SEQ], "sd:final")
            own()
            do(V.tensor_tensor(rl[:, 0:SEQ], ss[:, 0:SEQ], ss[:, 0:SEQ], ALU.mult))
            own()
            do(V.tensor_tensor(var[:, 0:SEQ], m[:, 0, 0:SEQ], rl[:, 0:SEQ], ALU.mult))
            own()
            do(V.tensor_scalar(var[:, 0:SEQ], var[:, 0:SEQ], EPS, None, ALU.add), "var:b2")
            rsqrt(rs[:, 0:SEQ], var[:, 0:SEQ], sd[:, 0:SEQ], "sd:b2")
            own()
            do(V.tensor_tensor(rs[:, 0:SEQ], rs[:, 0:SEQ], ss[:, 0:SEQ], ALU.mult))
            own()

            for f in range(NH):
                scaled((q2, k2)[f // 4][:, f % 4, :], f"qk:{f}", SEQ)
                do(V.scalar_tensor_tensor(x2[:, f, :], x2[:, f, :], gcol("final_norm", f), ss[:, 0:SEQ],
                                          ALU.mult, ALU.mult))
                if f == 5:
                    on_pe("rcol")
                    do(V.tensor_copy(small[:, 0:NT], slot("rcol", SEQ)[:, 0:NT]), "rd:rcol")
            hrows = slice(0, 2 * NH)
            on_pe(f"st:qk:{NH - 1}")
            do(V.tensor_scalar(var[hrows, 0:SEQ], ps[hrows, 1, :], 1.0 / DV, EPS, ALU.mult, ALU.add), "var:qk")
            rsqrt(rl[hrows, 0:SEQ], var[hrows, 0:SEQ], sd[hrows, 0:SEQ], "sd:qk")
            C.also("dve", "hr")
            do(V.memset(hb[:, :, 0:CONV - 1], 0.0))
            do(V.memset(xc[:, :, 0:SCW - 1], 0.0))
            do(V.memset(qpad[DV:P, :], 0.0))

            def head_norm(a, b):
                for f in range(a, b):
                    on_pe(f"hr:{f}")
                    t = (q2, k2)[f // 4][:, f % 4, :]
                    do(V.scalar_tensor_tensor(t, t, gcol(("q_norm_g_2", "k_norm_g_2")[f // 4], 0),
                                              ps[:, f % 3 * 2 + 3, :], ALU.mult, ALU.mult), f"qkn{f}")

            own()
            do(V.tensor_tensor(rs2[:, 0:SEQ], rs[:, 0:SEQ], rs[:, 0:SEQ], ALU.mult))
            head_norm(0, 6)
            C.also("dve", "qz0")
            for t in range(NT):
                on_pe(f"v:{t}")
                do(V.tensor_scalar(v2[:, t, :], slot(f"v:{t}", SEQ), small[:, t:t + 1], None, ALU.mult),
                   f"rd:v:{t}")
                if t == NT - 2:
                    head_norm(6, NH)

            def cf(n):
                own()
                for e in range(2):
                    scaled((t1, t2)[n % 2][:, e, 0:SEQ], f"cf:{2 * n + e}", SEQ)

            def gated(n):
                for e in range(2):
                    on_act(f"sig:cf:{2 * n + e}")
                    do(V.tensor_tensor(hb[:, n - 1 + e, CONV - 1:], t1[:, e, 0:SEQ], m[:, e, 0:SEQ], ALU.mult),
                       f"hb{n - 1 + e}")
                inputs[0] = n + 1
                own()

            tap_order = [(tap, c) for c in range(1, CT) for tap in range(CONV)]
            tap_done, inputs = [0], [0]

            def taps(n):
                for tap, c in tap_order[tap_done[0]:tap_done[0] + n]:
                    if c >= inputs[0]:
                        return
                    tap_done[0] += 1
                    wt = gcol("conf_dw_w_2", tap * CT + c)
                    name = f"conv{tap}:{c}"
                    if tap == 0:
                        do(V.tensor_scalar(conv[:, c, :], hb[:, c, 0:SEQ], wt, gcol("conf_dw_b_2", c),
                                           ALU.mult, ALU.add), name)
                    else:
                        own(f"conv{tap - 1}:{c}")
                        do(V.scalar_tensor_tensor(conv[:, c, :], hb[:, c, tap:tap + SEQ], wt, conv[:, c, :],
                                                  ALU.mult, ALU.add), name)

            def sc(n):
                p, part = n // 3, n % 3
                own()
                for e in range(2):
                    name = f"sc:{2 * n + e}"
                    if part == 1:
                        on_pe(name)
                        do(V.tensor_tensor(xc[:, e, SCW - 1:], slot(name, SEQ), t1[:, e, 0:SEQ], ALU.mult), "rd:" + name)
                    elif part == 0:
                        on_pe(name)
                        do(V.tensor_tensor(t1[:, e, 0:SEQ], slot(name, SEQ), rs2[:, 0:SEQ], ALU.mult), "rd:" + name)
                    else:
                        scaled(t1[:, e, 0:SEQ], name, SEQ)
                own()
                if part == 1:
                    for tap in range(SCW):
                        for e in range(2):
                            r = tap * CT + 2 * p + e
                            wt = gcol("sc_conv_w_2", r)
                            if tap == 0:
                                do(V.tensor_scalar(m[:, e, 0:SEQ], xc[:, e, 0:SEQ], wt, None, ALU.mult))
                            else:
                                do(V.scalar_tensor_tensor(m[:, e, 0:SEQ], xc[:, e, tap:tap + SEQ], wt,
                                                          m[:, e, 0:SEQ], ALU.mult, ALU.add))
                        own()
                elif part == 2:
                    for e in range(2):
                        do(V.tensor_tensor(hcr[:, 2 * p + e, :], t1[:, e, 0:SEQ], m[:, e, 0:SEQ], ALU.mult))

            ahead = {"z": 0, "r": 7, "o": 10}
            since = "z"
            behind = None
            gates = None
            for what, *at_ in blend_order() + [("end",)]:
                since = what if what in ahead else since
                if what == "r":
                    hd, = at_
                    for j in reversed(range(NT)):
                        on_act(f"ln{hd}:{j}")
                        do(V.scalar_tensor_tensor(spl(j), ps[:, 2 * j + 1, 0:SEQ - j * P], 0.0, spl(j),
                                                  ALU.max, ALU.add), f"sp{hd}:{j}")
                        if j == NT - 1:
                            C.also("dve", f"later{hd}:{j - 1}")
                        elif j:
                            own()
                            parts = later(j)
                            for n, (o, t) in enumerate(parts):
                                to = later(j - 1)[1][1][:, o - P:o - P + t.shape[-1]]
                                do(V.tensor_tensor(to, t, spl(j)[:, o:o + t.shape[-1]], ALU.add),
                                   *([f"later{hd}:{j - 1}"] if n == len(parts) - 1 else []))
                elif what == "o":
                    hd, = at_
                    r = slice(hd % 2 * DV, hd % 2 * DV + DV)
                    on_pe(f"o2:{hd}")
                    do(V.tensor_copy(o2[r, hd // 2, :], ps[r, 2 * NT - 1, :]), f"rd:o2:{hd}")
                    if hd + 1 < NH:
                        do(V.memset(qpad[r, :], 0.0), f"qz{hd + 1}")
                if gates is not None and what in ("r", "o"):
                    gated(gates)
                    gates = None
                if behind:
                    if behind[0] == "cf" and behind[1] % 2:
                        gates = behind[1]
                    (cf if behind[0] == "cf" else sc)(behind[1])
                    behind = None
                if what == "z" and hd % 2 == 0 and hd or what == "end":
                    c = hd // 2 - 1 if what == "z" else CT - 1
                    on_act(f"o2h{c}")
                    do(V.tensor_tensor(o2L[:, c, :], o2[:, c, :], f32(o2H[:, c, :]), ALU.subtract), f"o2l{c}")
                if what in ("cf", "sc"):
                    n, e, f = at_
                    taps(ahead[since])
                    if e == f == 1:
                        behind = (what, n)
            taps(CONV * CT)

            def layer_norm(p):
                if p == 1:
                    on_pe("st:mean")
                    for c in range(CT):
                        do(V.scalar_tensor_tensor(conv[:, c, :], slot("st:mean", SEQ), -1.0 / CW, conv[:, c, :],
                                                  ALU.mult, ALU.add),
                           *([f"cm:{c}"] + (["rd:st:mean"] if c == CT - 1 else [])))
                    for c in range(CT):
                        add_square("ln", c, SEQ)
                elif p == 2:
                    variance("lnv", SEQ, CW)
                    rsqrt(rl[:, 0:SEQ], var[:, 0:SEQ], sd[:, 0:SEQ], "sd:ln")
                elif p == 3:
                    own()
                    for c in range(CT + 1):
                        if c < CT:
                            if c >= 2:
                                on_act(f"hbn{c - 2}")
                            do(V.tensor_tensor(lnt[:, c % 2, 0:SEQ], conv[:, c, :], rl[:, 0:SEQ], ALU.mult), f"ln:{c}")
                        if c:
                            on_act(f"hch{c - 1}")
                            do(V.tensor_tensor(hbL[:, c - 1, :], hbn[:, (c - 1) % 2, 0:SEQ], f32(hbH[:, c - 1, :]),
                                               ALU.subtract), f"hbl{c - 1}")
                            do(V.tensor_tensor(hcL[:, c - 1, :], hcr[:, c - 1, :], f32(hcH[:, c - 1, :]),
                                               ALU.subtract), f"hcl{c - 1}")

            for b in range(3):
                for p in range(4):
                    own()
                    for e in range(2):
                        scaled(t1[:, e, 0:SEQ], f"gate{b}:{2 * p + e}", SEQ)
                    for e in range(2):
                        d = 2 * p + e
                        name = f"y{b}:{d}"
                        on_act(f"sig{b}:{d}")
                        on_pe(name)
                        if b == 0:
                            do(V.tensor_tensor(merged[:, d, :], slot(name, SEQ), t2[:, e, 0:SEQ], ALU.mult), "rd:" + name)
                        else:
                            do(V.tensor_tensor(m[:, e, 0:SEQ], slot(name, SEQ), t2[:, e, 0:SEQ], ALU.mult), "rd:" + name)
                            own()
                            do(V.tensor_tensor(merged[:, d, :], merged[:, d, :], m[:, e, 0:SEQ], ALU.add),
                               *([f"mg:{d}"] if b == 2 else []))
                        if b == 2:
                            on_act(f"mgh:{d}")
                            do(V.tensor_tensor(mgL[:, d, :], merged[:, d, :], f32(mgH[:, d, :]), ALU.subtract),
                               f"mgl{d}")
                    if b == 0:
                        layer_norm(p + 1)
            for d in range(KD):
                on_pe(f"wo2:{d}")
                own()
                do(V.tensor_tensor(x2[:, d, :], slot(f"wo2:{d}", SEQ), x2[:, d, :], ALU.add),
                   f"rd:wo2:{d}", f"h:f4:{d}")
                if d:
                    prep("f4", d - 1, ("ffn_norm_g_2",), SEQ)
            prep("f4", KD - 1, ("ffn_norm_g_2",), SEQ)
            ffn(4)


def _constants():
    c = np.zeros((P, C_MAIN), np.float32)
    r = np.arange(P)
    c[:, C_ID:C_ID + P] = np.eye(P)
    c[:, C_NTRI:C_NTRI + P] = -(r[:, None] >= r[None, :]).astype(np.float32)
    c[:, C_NONE:C_NONE + P] = -1.0
    c[:, C_ONE:C_ONE + P] = 1.0
    for f in range(NH):
        for e in range(2):
            c[e * DV:(e + 1) * DV, C_HEAD + f * 2 * NH + 2 * f + e] = 1.0
    c[:, C_MASK:C_MASK + P] = np.where(r[:, None] >= r[None, :], NEG, 0.0)
    bands = np.zeros((P, len(POOL_W), BAND), np.float32)
    for g, win in enumerate(POOL_W):
        def weight(step, count):
            return np.where((step >= 0) & (step < win), np.float32(1.0) / count, 0.0) - (step == 0)

        step = r[None, :] - r[:, None]
        bands[:, g, 0:P] = weight(step, np.minimum(r[None, :] + 1, win).astype(np.float32))
        bands[:, g, P:2 * P] = weight(step, np.float32(win))
    t = np.ones((P, 3, T1), np.float32)
    inv = np.float32(1.0) / np.power(np.float32(10000.0), np.arange(0, DR, 2, dtype=np.float32) / np.float32(DR))
    ang = np.arange(T1, dtype=np.float32)[None, :] * inv.astype(np.float32)[:, None]
    cos, sin = np.cos(ang), np.sin(ang)
    for p in range(P):
        sign = -1.0 if p % DR < DR // 2 else 1.0
        t[p, TAB_COS] = cos[p % (DR // 2)]
        t[p, TAB_SIN] = sign * sin[p % (DR // 2)]
    t[:, TAB_Q] *= np.float32(SM_SCALE)
    t[DN:DQK, TAB_Q] *= t[DN:DQK, TAB_COS]
    t[DQK:, TAB_Q] *= t[DQK:, TAB_SIN]
    heads = (np.arange(2 * NH * DV)[None, :] // DV == np.arange(2 * NH)[:, None]).astype(np.float32)
    return {"bands": bands, "consts": c, "tables": t, "heads": heads}


def _layout(inputs):
    a = {n: np.ascontiguousarray(v) for n, v in inputs.items()}
    gains = []
    for n, (_, k) in GAIN.items():
        v = a.pop(n).reshape(-1)
        gains.append(np.tile(v, k * P // v.size).reshape(k, P).T)
    a["gains"] = np.ascontiguousarray(np.concatenate(gains, axis=1))
    tokens = np.concatenate([a.pop("meta_tokens"), a.pop("x")[0]])
    a["tokens"] = np.ascontiguousarray(tokens.T.reshape(KD, P, T1).transpose(1, 0, 2))
    rope, half = np.arange(DR), np.roll(np.arange(DR), DR // 2)
    a["w_dkv"] = a["w_dkv"][:, np.concatenate([np.arange(RKV)] + [RKV + rope] * 2 + [RKV + half] * 2)]
    head = np.concatenate([np.arange(DN), DN + rope, DN + half])
    a["w_uq"] = a["w_uq"][0][:, (np.arange(NH)[:, None] * DQK + head).reshape(-1)]
    return {n: np.ascontiguousarray(v) for n, v in a.items()}


def kernel(**inputs):
    import concourse.bacc as _bacc
    from concourse.bass_utils import run_bass_kernel_spmd as _run

    arrays = {**_layout(inputs), **_constants()}

    def build(C):
        nc = _bacc.Bacc("TRN2", target_bir_lowering=False, num_devices=1)
        w = {n: nc.dram_tensor(f"in_{n}", a.shape, F32, kind="ExternalInput").ap() for n, a in arrays.items()}
        out = nc.dram_tensor("out", (KD, P, SEQ), F32, kind="ExternalOutput").ap()
        program(nc, w, out, C)
        return nc

    C = Counts()
    build(C)
    C.known = True
    nc = build(C)
    r = _run(nc, [{f"in_{n}": a for n, a in arrays.items()}], core_ids=[0])
    return np.ascontiguousarray(np.asarray(r.results[0]["out"]).reshape(D, SEQ).T)[None]
```
